# Optimizing a Trainium2 kernel written in Bass

```python
import jax, jax.numpy as jnp
from jax import lax
import numpy as np

D_MODEL = 2048
BATCH = 1
SEQ = 256
DEPTH = 2
DEC_BATCH = 1
DEC_SEQ = 32
PAST_LEN = 128

CHUNK = 64
SUB = 16
N_MIXERS = 2
N_HG_LAYERS = (DEPTH + 1) // 2
N_MLA_LAYERS = DEPTH // 2
HG_EXPAND = 128
HG_HEADS = D_MODEL // HG_EXPAND
HG_DK = HG_EXPAND
HG_DV = D_MODEL // HG_HEADS
HG_DIM = HG_HEADS * HG_DK
MLA_HEADS = 16
Q_LORA = 512
KV_LORA = 512
NOPE_DIM = 128
ROPE_DIM = 64
V_DIM = 128
ROPE_BASE = 10000.0
Q_BLOCK = 128
D_FF = 5632
CONV_K = 3
EPS = 1e-6

kernel_name = 'hybrid_hgrn2_mla_convffn_stream_step'

F32 = jnp.float32

def rms_norm(x, w):
    xf = x.astype(F32)
    y = xf * lax.rsqrt(jnp.mean(xf * xf, axis=-1, keepdims=True) + EPS)
    return (y * w.astype(F32)).astype(x.dtype)

def _gla_chunk(S, inp):
    q, k, v, logf = inp
    B, H, C, dk = q.shape
    ns = C // SUB
    b = jnp.cumsum(logf, axis=2)
    bs = b.reshape(B, H, ns, SUB, dk)
    qs = q.reshape(B, H, ns, SUB, dk)
    ks = k.reshape(B, H, ns, SUB, dk)
    vs = v.reshape(B, H, ns, SUB, -1)
    ref = jnp.concatenate([jnp.zeros_like(bs[:, :, :1, -1]), bs[:, :, :-1, -1]], axis=2)
    q_ref = qs * jnp.exp(bs - ref[:, :, :, None])
    blk = jnp.arange(ns)
    earlier = blk[None, :] < blk[:, None]
    expo = ref[:, :, :, None, None, :] - bs[:, :, None]
    k_ref = ks[:, :, None] * jnp.exp(jnp.where(earlier[:, :, None, None], expo, -jnp.inf))
    a_off = jnp.einsum('bhitk,bhijuk->bhitju', q_ref, k_ref)
    o = jnp.einsum('bhitju,bhjuv->bhitv', a_off, vs)
    pos = jnp.arange(SUB)
    causal = pos[None, :] <= pos[:, None]
    d_expo = bs[:, :, :, :, None, :] - bs[:, :, :, None, :, :]
    decay = jnp.exp(jnp.where(causal[:, :, None], d_expo, -jnp.inf))
    a_diag = jnp.einsum('bhitk,bhituk,bhiuk->bhitu', qs, decay, ks)
    o = o + jnp.einsum('bhitu,bhiuv->bhitv', a_diag, vs)
    o = o.reshape(B, H, C, -1) + jnp.einsum('bhck,bhkv->bhcv', q * jnp.exp(b), S)
    b_last = b[:, :, -1]
    S_new = jnp.exp(b_last)[..., None] * S + jnp.einsum(
        'bhck,bhcv->bhkv', k * jnp.exp(b_last[:, :, None] - b), v)
    return S_new, o

def hgrn2_recurrence(q, k, v, logf, S0):
    B, H, L, _ = q.shape
    n = -(-L // CHUNK)
    padw = ((0, 0), (0, 0), (0, n * CHUNK - L), (0, 0))
    q, k, v, logf = (jnp.pad(t, padw) for t in (q, k, v, logf))
    to_chunks = lambda t: jnp.moveaxis(t.reshape(B, H, n, CHUNK, t.shape[-1]), 2, 0)
    S, o = lax.scan(_gla_chunk, S0, (to_chunks(q), to_chunks(k), to_chunks(v), to_chunks(logf)))
    o = jnp.moveaxis(o, 0, 2).reshape(B, H, n * CHUNK, -1)[:, :, :L]
    return o, S

def hgrn2_mixer(h, S0, w_in, g_norm_w, w_out, lb):
    B, L, _ = h.shape
    q, f, i, g = jnp.split(h @ w_in, 4, axis=-1)
    heads = lambda t, d: t.reshape(B, L, HG_HEADS, d).transpose(0, 2, 1, 3).astype(F32)
    q = jax.nn.silu(heads(q, HG_DK))
    lb = lb.astype(F32).reshape(HG_HEADS, 1, HG_DK)
    fg = lb + (1.0 - lb) * jax.nn.sigmoid(heads(f, HG_DK))
    k = 1.0 - fg
    logf = jnp.log(fg)
    v = heads(i, HG_DV)
    o, S = hgrn2_recurrence(q, k, v, logf, S0.astype(F32))
    o = o.transpose(0, 2, 1, 3)
    o = rms_norm(o, g_norm_w) * jax.nn.silu(g.reshape(B, L, HG_HEADS, HG_DV).astype(F32))
    y = o.reshape(B, L, HG_HEADS * HG_DV).astype(h.dtype) @ w_out
    return y, S.astype(h.dtype)

def rope(x, pos):
    half = ROPE_DIM // 2
    inv = ROPE_BASE ** (-jnp.arange(half, dtype=F32) / half)
    ang = pos[:, None] * inv[None]
    shape = (ang.shape[0],) + (1,) * (x.ndim - 3) + (half,)
    cos = jnp.cos(ang).reshape(shape)
    sin = jnp.sin(ang).reshape(shape)
    xf = x.astype(F32)
    x1, x2 = xf[..., :half], xf[..., half:]
    return jnp.concatenate([x1 * cos - x2 * sin, x2 * cos + x1 * sin], axis=-1).astype(x.dtype)

def chunk_causal_attention(q_nope, q_pe, k_nope, k_pe, v, q_chunk, k_chunk):
    B, Lq, H, _ = q_nope.shape
    blk = Q_BLOCK if Lq % Q_BLOCK == 0 else Lq
    nb = Lq // blk
    scale = (NOPE_DIM + ROPE_DIM) ** -0.5

    def one_block(args):
        qn, qp, qc = args
        s = jnp.einsum('bqhd,bkhd->bhqk', qn, k_nope) + jnp.einsum('bqhr,bkr->bhqk', qp, k_pe)
        s = s.astype(F32) * scale
        s = jnp.where(k_chunk[None, :] <= qc[:, None], s, -jnp.inf)
        p = jax.nn.softmax(s, axis=-1).astype(v.dtype)
        return jnp.einsum('bhqk,bkhv->bqhv', p, v)

    split = lambda t: jnp.moveaxis(t.reshape((B, nb, blk) + t.shape[2:]), 1, 0)
    o = lax.map(one_block, (split(q_nope), split(q_pe), q_chunk.reshape(nb, blk)))
    return jnp.moveaxis(o, 0, 1).reshape(B, Lq, H, -1)

def mla_mixer(h, ckv_cache, kpe_cache, past, w_down, q_norm_w, kv_norm_w, w_uq, w_ukv, w_out):
    B, L, _ = h.shape
    qpos = past + jnp.arange(L)
    pos_f = qpos.astype(F32)
    down = h @ w_down
    c_q = rms_norm(down[..., :Q_LORA], q_norm_w)
    c_kv = rms_norm(down[..., Q_LORA:Q_LORA + KV_LORA], kv_norm_w)
    k_pe = rope(down[..., Q_LORA + KV_LORA:], pos_f)
    q = (c_q @ w_uq).reshape(B, L, MLA_HEADS, NOPE_DIM + ROPE_DIM)
    q_nope = q[..., :NOPE_DIM]
    q_pe = rope(q[..., NOPE_DIM:], pos_f)
    if ckv_cache is None:
        ckv_all, kpe_all = c_kv, k_pe
    else:
        ckv_all = jnp.concatenate([ckv_cache.astype(c_kv.dtype), c_kv], axis=1)
        kpe_all = jnp.concatenate([kpe_cache.astype(k_pe.dtype), k_pe], axis=1)
    Lk = ckv_all.shape[1]
    kv = (ckv_all @ w_ukv).reshape(B, Lk, MLA_HEADS, NOPE_DIM + V_DIM)
    k_nope, v = kv[..., :NOPE_DIM], kv[..., NOPE_DIM:]
    o = chunk_causal_attention(q_nope, q_pe, k_nope, kpe_all, v,
                               qpos // CHUNK, jnp.arange(Lk) // CHUNK)
    y = o.reshape(B, L, MLA_HEADS * V_DIM) @ w_out
    return y, c_kv, k_pe

def conv_ffn(h, buf, w_in, conv_w, conv_b, w_out):
    L = h.shape[1]
    u = h @ w_in
    ext = jnp.concatenate([buf.astype(u.dtype), u], axis=1)
    c = conv_b
    for j in range(CONV_K):
        c = c + conv_w[j] * ext[:, j:j + L]
    gate, up = jnp.split(c, 2, axis=-1)
    y = (jax.nn.silu(gate) * up) @ w_out
    return y, ext[:, L:]

def trunk(x, hg_states, ckv_caches, kpe_caches, conv_states, lower_bounds, norm_w,
          hgrn_w_in, hgrn_gnorm_w, hgrn_w_out, mla_w_down, mla_q_norm_w, mla_kv_norm_w,
          mla_w_uq, mla_w_ukv, mla_w_out, ffn_w_in, ffn_conv_w, ffn_conv_b, ffn_w_out):
    past = 0 if ckv_caches is None else ckv_caches.shape[2]
    new_hg, new_ckv, new_kpe, new_conv = [], [], [], []
    for layer in range(DEPTH):
        idx = layer // N_MIXERS
        h = rms_norm(x, norm_w[layer, 0])
        if layer % N_MIXERS == 0:
            m, s = hgrn2_mixer(h, hg_states[idx], hgrn_w_in[idx], hgrn_gnorm_w[idx],
                               hgrn_w_out[idx], lower_bounds[layer])
            new_hg.append(s)
        else:
            m, c, kp = mla_mixer(h,
                                 None if ckv_caches is None else ckv_caches[idx],
                                 None if kpe_caches is None else kpe_caches[idx],
                                 past, mla_w_down[idx], mla_q_norm_w[idx], mla_kv_norm_w[idx],
                                 mla_w_uq[idx], mla_w_ukv[idx], mla_w_out[idx])
            new_ckv.append(c)
            new_kpe.append(kp)
        x = x + rms_norm(m, norm_w[layer, 1])
        f, buf = conv_ffn(rms_norm(x, norm_w[layer, 2]), conv_states[layer], ffn_w_in[layer],
                          ffn_conv_w[layer], ffn_conv_b[layer], ffn_w_out[layer])
        new_conv.append(buf)
        x = x + rms_norm(f, norm_w[layer, 3])
    return x, jnp.stack(new_hg), jnp.stack(new_ckv), jnp.stack(new_kpe), jnp.stack(new_conv)

def setup_inputs(seed: int = 0) -> dict:
    key = jax.random.key(seed)
    ks = jax.random.split(key, 24)
    nrm = lambda k, shape, scale: jax.random.normal(k, shape, F32) * scale
    gain = lambda k, shape: 1.0 + 0.05 * jax.random.normal(k, shape, F32)
    return {
        'x_prompt': nrm(ks[0], (BATCH, SEQ, D_MODEL), 1.0),
        'x_sample': nrm(ks[1], (DEC_BATCH, DEC_SEQ, D_MODEL), 1.0),
        'state_hgrn': nrm(ks[2], (N_HG_LAYERS, DEC_BATCH, HG_HEADS, HG_DK, HG_DV), 0.5),
        'cache_ckv': nrm(ks[3], (N_MLA_LAYERS, DEC_BATCH, PAST_LEN, KV_LORA), 1.0),
        'cache_kpe': nrm(ks[4], (N_MLA_LAYERS, DEC_BATCH, PAST_LEN, ROPE_DIM), 1.0),
        'state_conv': nrm(ks[5], (DEPTH, DEC_BATCH, CONV_K - 1, 2 * D_FF), 1.0),
        'norm_w': gain(ks[6], (DEPTH, 4, D_MODEL)),
        'lb_logits': nrm(ks[7], (DEPTH + 1, HG_DIM), 0.1),
        'hgrn_w_in': nrm(ks[8], (N_HG_LAYERS, D_MODEL, 4 * HG_DIM), D_MODEL ** -0.5),
        'hgrn_gnorm_w': gain(ks[9], (N_HG_LAYERS, HG_DV)),
        'hgrn_w_out': nrm(ks[10], (N_HG_LAYERS, HG_HEADS * HG_DV, D_MODEL), (HG_HEADS * HG_DV) ** -0.5),
        'mla_w_down': nrm(ks[11], (N_MLA_LAYERS, D_MODEL, Q_LORA + KV_LORA + ROPE_DIM), D_MODEL ** -0.5),
        'mla_q_norm_w': gain(ks[12], (N_MLA_LAYERS, Q_LORA)),
        'mla_kv_norm_w': gain(ks[13], (N_MLA_LAYERS, KV_LORA)),
        'mla_w_uq': nrm(ks[14], (N_MLA_LAYERS, Q_LORA, MLA_HEADS * (NOPE_DIM + ROPE_DIM)), Q_LORA ** -0.5),
        'mla_w_ukv': nrm(ks[15], (N_MLA_LAYERS, KV_LORA, MLA_HEADS * (NOPE_DIM + V_DIM)), KV_LORA ** -0.5),
        'mla_w_out': nrm(ks[16], (N_MLA_LAYERS, MLA_HEADS * V_DIM, D_MODEL), (MLA_HEADS * V_DIM) ** -0.5),
        'ffn_w_in': nrm(ks[17], (DEPTH, D_MODEL, 2 * D_FF), D_MODEL ** -0.5),
        'ffn_conv_w': nrm(ks[18], (DEPTH, CONV_K, 2 * D_FF), CONV_K ** -0.5),
        'ffn_conv_b': nrm(ks[19], (DEPTH, 2 * D_FF), 0.02),
        'ffn_w_out': nrm(ks[20], (DEPTH, D_FF, D_MODEL), D_FF ** -0.5),
    }

def reference(x_prompt, x_sample, state_hgrn, cache_ckv, cache_kpe, state_conv, norm_w, lb_logits,
              hgrn_w_in, hgrn_gnorm_w, hgrn_w_out, mla_w_down, mla_q_norm_w, mla_kv_norm_w,
              mla_w_uq, mla_w_ukv, mla_w_out, ffn_w_in, ffn_conv_w, ffn_conv_b, ffn_w_out):
    lower_bounds = jnp.cumsum(jax.nn.softmax(lb_logits.astype(F32), axis=0), axis=0)
    bp = x_prompt.shape[0]
    hg0 = jnp.zeros((N_HG_LAYERS, bp, HG_HEADS, HG_DK, HG_DV), x_prompt.dtype)
    conv0 = jnp.zeros((DEPTH, bp, CONV_K - 1, 2 * D_FF), x_prompt.dtype)
    y_prompt, hg_p, ckv_p, kpe_p, conv_p = trunk(
        x_prompt, hg0, None, None, conv0, lower_bounds, norm_w,
        hgrn_w_in, hgrn_gnorm_w, hgrn_w_out, mla_w_down, mla_q_norm_w, mla_kv_norm_w,
        mla_w_uq, mla_w_ukv, mla_w_out, ffn_w_in, ffn_conv_w, ffn_conv_b, ffn_w_out)
    y_sample, hg_s, ckv_s, kpe_s, conv_s = trunk(
        x_sample, state_hgrn, cache_ckv, cache_kpe, state_conv, lower_bounds, norm_w,
        hgrn_w_in, hgrn_gnorm_w, hgrn_w_out, mla_w_down, mla_q_norm_w, mla_kv_norm_w,
        mla_w_uq, mla_w_ukv, mla_w_out, ffn_w_in, ffn_conv_w, ffn_conv_b, ffn_w_out)
    return (y_prompt, y_sample, hg_p, hg_s, ckv_p, ckv_s, kpe_p, kpe_s, conv_p, conv_s)


_drawn_inputs = setup_inputs


def setup_inputs(seed=0):
    import zlib

    import numpy as np

    out = dict(_drawn_inputs(seed))
    spreads = {}
    factors = {}
    for name, (base, spread) in spreads.items():
        noise = np.random.default_rng([zlib.crc32(name.encode()), seed]).standard_normal(out[name].shape)
        drawn = base * np.exp(spread * noise) if base else spread * noise
        out[name] = __import__('jax').numpy.asarray(drawn.astype(out[name].dtype))
    for name, factor in factors.items():
        out[name] = (out[name] * factor).astype(out[name].dtype)
    return out
```

```python
import math
from contextlib import ExitStack

import concourse.bass as bass
from concourse import mybir

F32 = mybir.dt.float32
F32R = mybir.dt.float32r
ALU = mybir.AluOpType
ACT = mybir.ActivationFunctionType
AX_X = mybir.AxisListType.X

P = 128
TP = 256
TS = 32
T = TP + TS
PAST = 128
TK = TP + PAST + TS
EPS = 1e-6
LEVELS = 7
RING = 4
UNITS = 8
LATENT = 4
EXP_LN_SET = 6
SILU_SET = 18
EXP_MAX = 2.0 ** 63
NEGATIVE = -1e30


def pieces(kt):
    return [(a, min(UNITS, kt - a)) for a in range(0, kt, UNITS)]


def trunk_program(nc, a):
    D = a["x"].shape[1] * P
    KT = D // P
    HEADS = KT
    FT = 2 * (a["w_fo"].shape[2] // P)
    HF = FT // 2
    PAIRS = HEADS // 2
    SCALE = float(P + 64) ** -0.5
    PK, PH = pieces(KT), pieces(HF)
    assert HF % 2 == 0 and KT % 4 == 0

    gemm4 = [(t, s, n) for t in range(4) for s, n in PK]
    out4 = [(t, s, n) for t in range(4) for s, n in PH]
    order = [("hgrn_in", HEADS, gemm4, 4), ("hgrn_out", KT // 4, gemm4, 4)]
    for layer in range(2):
        if layer == 1:
            order += [("down", 2, gemm4, 4), ("down_last", 1, [(0, s, n) for s, n in PK], 1),
                      ("pairs", PAIRS, [(0, 0, 8), (1, 8, 4), (2, 0, 8), (3, 8, 8)], 7),
                      ("mla_out", KT // 4, gemm4, 4)]
        for half in range(2):
            order += [(f"ffn_in{layer}{half}", HF // 2, gemm4, 4), (f"ffn_out{layer}{half}", KT // 4, out4, 4)]
    chunk0, tile0, c, t = {}, {}, 0, 0
    for name, trips, chunks, tiles in order:
        chunk0[name], tile0[name] = c, t
        c, t = c + trips * len(chunks), t + trips * tiles
    CHUNKS = {name: chunks for name, _, chunks, _ in order}
    TILES = {name: tiles for name, _, _, tiles in order}

    class Chunk:
        def __init__(self, phase, i, k):
            n = len(CHUNKS[phase])
            at = chunk0[phase] + k
            self.first = isinstance(i, int) and at + i * n < RING
            self.slot = (at + (i * n if isinstance(i, int) else 0)) % RING
            assert isinstance(i, int) or n % RING == 0
            self.number = i * n + at
            if isinstance(i, int):
                self.load = (at + i * n) // RING
            else:
                self.load = i * (n // RING) + at // RING
            self.tile, self.start, self.units = CHUNKS[phase][k]

    def tile_number(phase, i, t):
        return i * TILES[phase] + (tile0[phase] + t)

    with ExitStack() as ctx:
        def sb(name, shape, dt=F32):
            return ctx.enter_context(nc.sbuf_tensor(name, shape, dt))

        def sem(name):
            return ctx.enter_context(nc.semaphore(name))

        psum = [ctx.enter_context(nc.psum_tensor(f"bank{n}", [P, 512], F32)) for n in range(8)]

        raw = sb("raw", [P, RING, UNITS * P])
        w_hi = sb("w_hi", [P, RING, UNITS * P], F32R)
        w_lo = sb("w_lo", [P, RING, UNITS * P], F32R)
        X = sb("X", [P, KT, T])
        h_hi = sb("h_hi", [P, max(KT * T, LATENT * (T + TK))], F32R)
        h_lo = sb("h_lo", [P, max(KT * T, LATENT * (T + TK))], F32R)
        taken = {"mixer": 0, "ffn": 0}
        with ExitStack() as mixer:
            def sbm(name, shape, dt=F32):
                taken["mixer"] += 4 * math.prod(shape[1:])
                return mixer.enter_context(nc.sbuf_tensor(name, shape, dt))
            o_hi = sbm("o_hi", [P, KT, T], F32R)
            o_lo = sbm("o_lo", [P, KT, T], F32R)
            row_tiles = sbm("row_tiles", [P, 10, T])
            qraw, graw, vfm, key, query, gate, fgate, qb, ke, diag = (row_tiles[:, n, :] for n in range(10))
            vtok, ktok = sbm("vtok", [P, 3, P]), sbm("ktok", [P, 3, P])
            lev = sbm("lev", [P, 2, LEVELS * 64])
            lev_s = sbm("lev_s", [TS, 5, 16])
            s_old, s_mid = sbm("s_old", [P, P]), sbm("s_mid", [P, P])
            s_new = sbm("s_new", [P, 2, P])
        EXT = T + 4
        with ExitStack() as ffn:
            def sbf(name, shape, dt=F32):
                taken["ffn"] += 4 * math.prod(shape[1:])
                return ffn.enter_context(nc.sbuf_tensor(name, shape, dt))
            g_hi = sbf("g_hi", [P, HF, T], F32R)
            g_lo = sbf("g_lo", [P, HF, T], F32R)
            ext = sbf("ext", [P, 4, EXT])
            cv = sbf("cv", [P, 4, T + 2])
            prod = sbf("prod", [P, 2, T])
        sb("shared", [P, max(taken.values()) // 4])
        Y = sb("Y", [P, max(KT, 16), T])
        yt = sb("yt", [P, 4, T])
        ssq = sb("ssq", [P, T])
        ones = sb("ones", [P, P])
        ident = sb("ident", [P, P])
        swap = sb("swap", [P, P])
        cos = sb("cos", [P, T])
        sin = sb("sin", [P, T])
        chunk_mask = sb("chunk_mask", [P, 3 * P])
        level_mask_f = sb("level_mask", [P, LEVELS, 64])
        level_mask = level_mask_f[:].rearrange("p l t -> p (l t)")
        carry = sb("carry", [P, T])
        eps = sb("eps", [P, 1])
        norm_w = sb("norm_w", [P, 2, 4, KT])
        lat_w = sb("lat_w", [P, 2, LATENT])
        gnorm_w = sb("gnorm_w", [P, 1])
        lbl = sb("lbl", [P, 3, HEADS])
        lbt = sb("lbt", [P, 4, HEADS])
        lb = sb("lb", [P, HEADS])
        oml = sb("oml", [P, HEADS])
        conv_w = sb("conv_w", [P, 2, 2 * FT, 4])
        conv_old = sb("conv_old", [P, 2, 2 * FT, 2])
        conv_new = sb("conv_new", [P, 2 * FT, 4])
        small = sb("small", [P, 3, T])

        LR, RSA, RSB = small[:, 0, :], small[:, 1, :], small[:, 2, :]
        H_HI = h_hi[:, 0:KT * T].rearrange("p (k t) -> p k t", t=T)
        H_LO = h_lo[:, 0:KT * T].rearrange("p (k t) -> p k t", t=T)

        loaded = [sem(f"loaded{n}") for n in range(RING)]
        consts_in = sem("consts_in")
        x_in = sem("x_in")
        hi_done, lo_done, chunk_done = sem("hi_done"), sem("lo_done"), sem("chunk_done")
        evacuated = sem("evacuated")
        filled = sem("filled")
        block = None

        def ring_load(sp, w, phase, i, k, index):
            ch = Chunk(phase, i, k)
            if not ch.first:
                sp.wait_ge(lo_done, ch.number - (RING - 1))
            src = w[bass.ds(index, 1), :, ch.start * P:(ch.start + ch.units) * P].rearrange("a p n -> p (a n)")
            sp.dma_start(raw[:, ch.slot, 0:ch.units * P], src).then_inc(loaded[ch.slot], 16)

        def split_hi(act, phase, i, k):
            ch = Chunk(phase, i, k)
            act.wait_ge(loaded[ch.slot], 16 * (ch.load + 1))
            if not ch.first:
                act.wait_ge(chunk_done, ch.number - (RING - 1))
            n = ch.units * P
            act.activation(w_hi[:, ch.slot, 0:n], raw[:, ch.slot, 0:n], ACT.Copy).then_inc(hi_done, 1)

        def split_lo(dve, phase, i, k):
            ch = Chunk(phase, i, k)
            dve.wait_ge(hi_done, ch.number + 1)
            n = ch.units * P
            dve.tensor_tensor(w_lo[:, ch.slot, 0:n], raw[:, ch.slot, 0:n], w_hi[:, ch.slot, 0:n].bitcast(F32),
                              ALU.subtract).then_inc(lo_done, 1)

        def product(pe, out, ch, unit, rhs_hi, rhs_lo, start, stop):
            w = slice(unit * P, (unit + 1) * P)
            pe.matmul(out, w_hi[:, ch.slot, w], rhs_hi, start=start, stop=False)
            pe.matmul(out, w_hi[:, ch.slot, w], rhs_lo, start=False, stop=False)
            return pe.matmul(out, w_lo[:, ch.slot, w], rhs_hi, start=False, stop=stop)

        def tile_chunks(phase, t):
            return [k for k, (tt, _, _) in enumerate(CHUNKS[phase]) if tt == t]

        def gemm_chunk(pe, phase, i, k, hi, lo, kt):
            ch = Chunk(phase, i, k)
            if ch.start == 0 and not (isinstance(i, int) and i * TILES[phase] + ch.tile < 4):
                pe.wait_ge(evacuated, tile_number(phase, i, ch.tile) - 3)
            pe.wait_ge(lo_done, ch.number + 1)
            bank = psum[(ch.tile + (i * TILES[phase] if isinstance(i, int) else 0)) % 4]
            for u in range(ch.units):
                kk = ch.start + u
                mm = product(pe, bank[:, 0:T], ch, u, hi[:, kk, :], lo[:, kk, :], kk == 0, kk == kt - 1)
            mm.then_inc(chunk_done, 1)

        def last_chunk(phase, i, t):
            return Chunk(phase, i, tile_chunks(phase, t)[-1]).number + 1

        hg = ctx.enter_context(ExitStack())

        class HG:
            base = Y[:, :, :].rearrange("p k t -> p (k t)")
            Z = base[:, 0:LEVELS * T]
            o = LEVELS * T
            EX = base[:, o:o + 3 * T]
            SG = base[:, o + 3 * T:o + 6 * T]
            B = base[:, o + 6 * T:o + 7 * T]
            EB = base[:, o + 7 * T:o + 8 * T]
            EE = base[:, o + 8 * T:o + 9 * T]
        assert 16 * T >= (LEVELS + 9) * T
        on = yt[:, 0, :]
        o_sq = yt[:, 1, :]
        t1 = yt[:, 2, :]

        names = ["clamped", "logs", "sigmoids", "fgates", "keys", "gates", "logf", "decays", "ends_exp", "diffs",
                 "diffs_exp", "ke_ready", "pairs_ready", "v_turned", "v_tok", "k_turned", "k_tok", "levels_done",
                 "att_ready", "updates", "mid_state", "states", "o_raw", "o_squared", "o_summed", "o_logs", "o_rstd", "o_scaled",
                 "o_ready", "o_hi", "o_done", "s_loaded", "s_stored", "lb_ready"]
        S = {n: sem("h_" + n) for n in names}
        TR, LVA, LVB, DG = psum[4], psum[5], psum[6], psum[7]
        OV, SU, GS = psum[7], psum[5], psum[6]
        BLOCKS = [(0, P), (P, P), (TP, TS)]

        def halves(ap, m):
            v = ap.rearrange("p (b two m) -> p b two m", two=2, m=m)
            return v[:, :, 0, :], v[:, :, 1, :]

        def ref_col(m, n):
            v = HG.B[:, 0:n].rearrange("p (b two m) -> p b two m", two=2, m=m)
            return v[:, :, 0, m - 1:m].to_broadcast([P, n // (2 * m), m])

        def level_span(l):
            return T if 2 ** l < TS else TP

        IN = "hgrn_in"

        def on_position(split, eng, j, k):
            per = len(PK)
            if per == 2:
                split(eng, IN, j, k)
            elif k % 2:
                split(eng, IN, j, k // 2)

        def hgrn_act(act, j, gemm, main, tail):
            r, t = j - 1, j - 2
            hi = (lambda k: on_position(split_hi, act, j, k)) if gemm else (lambda k: None)
            hi(0); hi(1)
            if main:
                act.wait_ge(chunk_done, last_chunk(IN, r, 2))
                if not isinstance(r, int) or r > 0:
                    act.wait_ge(S["v_turned"], r)
                act.activation(vfm[:], psum[2][:, 0:T], ACT.Copy).then_inc(evacuated, 1)
            hi(2); hi(3)
            if main:
                act.wait_ge(chunk_done, last_chunk(IN, r, 3))
                act.activation(graw[:], psum[3][:, 0:T], ACT.Copy)
                act.activation(HG.EX[:, 2 * T:3 * T], psum[3][:, 0:T], ACT.Exp, scale=-1.0).then_inc(evacuated, 1)
            if tail:
                act.wait_ge(S["k_turned"], t + 1)
                act.activation(ktok[:, 0:2, :], TR[:, 0:2 * P], ACT.Copy)
                act.activation(ktok[0:TS, 2, :], TR[0:TS, 2 * P:3 * P], ACT.Copy).then_inc(S["k_tok"], 1)
            hi(4)
            if main:
                act.wait_ge(S["clamped"], r + 1)
                act.activation(HG.SG, HG.EX, ACT.Ln, bias=1.0).then_inc(S["logs"], 1)
                act.wait_ge(S["logs"], r + 1)
                act.activation(HG.SG, HG.SG, ACT.Exp, scale=-1.0).then_inc(S["sigmoids"], 1)
            hi(5)
            if main:
                act.wait_ge(S["fgates"], r + 1)
                act.activation(fgate[:], fgate[:], ACT.Ln).then_inc(S["logf"], 1)
            hi(6)
            if tail:
                act.wait_ge(S["o_raw"], t + 1)
                act.activation(o_sq, OV[:, 0:T], ACT.Square).then_inc(S["o_squared"], 1)
                act.wait_ge(S["states"], t + 1)
                for n, out in enumerate((a["o_hp"], a["o_hs"])):
                    act.dma_start(out[bass.ds(t, 1), :, :].rearrange("h k v -> k (h v)"), s_new[:, n, :])\
                        .then_inc(S["s_stored"], 16)
                if not isinstance(t, int) or t < HEADS - 1:
                    state_load(act, t + 1)
            if main:
                act.wait_ge(S["v_turned"], r + 1)
                act.activation(vtok[:, 0:2, :], TR[:, 0:2 * P], ACT.Copy)
                act.activation(vtok[0:TS, 2, :], TR[0:TS, 2 * P:3 * P], ACT.Copy).then_inc(S["v_tok"], 1)
                act.wait_ge(S["decays"], r + 1)
                if not isinstance(r, int) or r > 0:
                    act.wait_ge(S["states"], r)
                act.activation(HG.EB, HG.B, ACT.Exp)
                for n, (b0, bn) in enumerate(BLOCKS):
                    e = act.activation(HG.EE[:, b0:b0 + bn], HG.B[:, b0:b0 + bn], ACT.Exp, scale=-1.0,
                                       bias=HG.B[:, b0 + bn - 1:b0 + bn])
                e.then_inc(S["ends_exp"], 1)
            hi(7)
            if main:
                act.wait_ge(S["diffs"], r + 1)
                act.activation(HG.Z[:, 0:5 * T], HG.Z[:, 0:5 * T], ACT.Exp)
                v = HG.Z[:, 5 * T:7 * T].rearrange("p (l t) -> p l t", l=2)[:, :, 0:TP]
                act.activation(v, v, ACT.Exp).then_inc(S["diffs_exp"], 1)
            if tail:
                act.wait_ge(S["o_summed"], t + 1)
                act.activation(LR, GS[:, 0:T], ACT.Ln, scale=1.0 / P, bias=eps[:, 0:1]).then_inc(S["o_logs"], 1)
                act.wait_ge(S["o_logs"], t + 1)
                act.activation(RSA, LR, ACT.Exp, scale=-0.5).then_inc(S["o_rstd"], 1)
            if gemm:
                act.wait_ge(chunk_done, last_chunk(IN, j, 0))
                if main:
                    act.wait_ge(S["gates"], r + 1)
                act.activation(HG.EX[:, 0:T], psum[0][:, 0:T], ACT.Exp, scale=-1.0).then_inc(evacuated, 1)
                act.wait_ge(chunk_done, last_chunk(IN, j, 1))
                act.activation(qraw[:], psum[1][:, 0:T], ACT.Copy)
                act.activation(HG.EX[:, T:2 * T], psum[1][:, 0:T], ACT.Exp, scale=-1.0).then_inc(evacuated, 1)
            if tail:
                act.wait_ge(S["o_ready"], t + 1)
                act.activation(o_hi[:, bass.ds(t, 1), :], on.unsqueeze(1), ACT.Copy).then_inc(S["o_hi"], 1)

        def hgrn_dve(dve, j, gemm, main, tail):
            r, t = j - 1, j - 2
            lo = (lambda k: on_position(split_lo, dve, j, k)) if gemm else (lambda k: None)
            lo(0); lo(1); lo(2); lo(3)
            if tail:
                dve.wait_ge(S["levels_done"], t + 1)
                for n, lv in enumerate((LVA, LVB)):
                    dve.tensor_tensor(lev[:, n, :], lv[:, 0:LEVELS * 64], level_mask, ALU.mult)
                dve.tensor_tensor(diag[:, 0:TP].rearrange("p (n t) -> p n t", n=2), DG[:, 0:TP].rearrange("p (n t) -> p n t", n=2),
                                  ident[:].unsqueeze(1).to_broadcast([P, 2, P]), ALU.mult)
                dve.tensor_tensor(diag[0:TS, TP:T], DG[0:TS, TP:T], ident[0:TS, 0:TS], ALU.mult)
                dve.tensor_tensor(lev_s[:], DG[0:TS, T:T + 5 * 16].rearrange("p (l t) -> p l t", l=5),
                                  level_mask_f[0:TS, 0:5, 0:16], ALU.mult).then_inc(S["att_ready"], 1)
            if main:
                dve.wait_ge(evacuated, tile_number(IN, r, 3) + 1)
                dve.tensor_scalar(HG.EX, HG.EX, EXP_MAX, None, ALU.min).then_inc(S["clamped"], 1)
            lo(4)
            if main:
                dve.wait_ge(S["sigmoids"], r + 1)
                dve.tensor_scalar(fgate[:], HG.SG[:, 0:T], oml[:, bass.ds(r, 1)], lb[:, bass.ds(r, 1)],
                                  ALU.mult, ALU.add).then_inc(S["fgates"], 1)
                if not isinstance(r, int) or r > 0:
                    dve.wait_ge(S["levels_done"], r)
                dve.scalar_tensor_tensor(out=key[:], in0=HG.SG[:, 0:T], scalar=oml[:, bass.ds(r, 1)],
                                         in1=HG.EX[:, 0:T], op0=ALU.mult, op1=ALU.mult)
                dve.tensor_tensor(query[:], qraw[:], HG.SG[:, T:2 * T], ALU.mult)
            lo(5)
            if tail:
                dve.wait_ge(S["updates"], t + 1)
                if not isinstance(t, int) or t > 0:
                    dve.wait_ge(S["s_stored"], 32 * t)
                    dve.wait_ge(S["o_raw"], t)
                dve.wait_ge(S["s_loaded"], 16 * (t + 1))
                dve.tensor_copy(s_mid[:], SU[:, 0:P]).then_inc(S["mid_state"], 1)
                dve.scalar_tensor_tensor(out=s_new[:, 1, :], in0=s_old[:], scalar=HG.EB[:, T - 1:T],
                                         in1=SU[:, 2 * P:3 * P], op0=ALU.mult, op1=ALU.add)
                dve.wait_ge(S["mid_state"], t + 1)
                dve.scalar_tensor_tensor(out=s_new[:, 0, :], in0=s_mid[:], scalar=HG.EB[:, TP - 1:TP],
                                         in1=SU[:, P:2 * P], op0=ALU.mult, op1=ALU.add).then_inc(S["states"], 1)
            if main:
                dve.wait_ge(S["logf"], r + 1)
                dve.tensor_tensor_scan(HG.B, carry[:], fgate[:], 0.0, ALU.mult, ALU.add).then_inc(S["decays"], 1)
            lo(6)
            if main:
                dve.wait_ge(S["decays"], r + 1)
                for l in range(LEVELS):
                    m, n = 2 ** l, level_span(l)
                    zf, zs = halves(HG.Z[:, l * T:l * T + n], m)
                    bf, bs = halves(HG.B[:, 0:n], m)
                    dve.tensor_tensor(zf, ref_col(m, n), bf, ALU.subtract)
                    z = dve.tensor_tensor(zs, bs, ref_col(m, n), ALU.subtract)
                z.then_inc(S["diffs"], 1)
            lo(7)
            if main:
                dve.wait_ge(S["ends_exp"], r + 1)
                dve.tensor_tensor(qb[:], query[:], HG.EB, ALU.mult)
                dve.tensor_tensor(ke[:], key[:], HG.EE, ALU.mult).then_inc(S["ke_ready"], 1)
            if tail:
                dve.wait_ge(S["o_rstd"], t + 1)
                dve.scalar_tensor_tensor(out=t1, in0=gate[:], scalar=gnorm_w[:, 0:1], in1=RSA,
                                         op0=ALU.mult, op1=ALU.mult).then_inc(S["o_scaled"], 1)
                dve.wait_ge(S["o_scaled"], t + 1)
                dve.tensor_tensor(on, t1, OV[:, 0:T], ALU.mult).then_inc(S["o_ready"], 1)
            if main:
                dve.tensor_tensor(gate[:], graw[:], HG.SG[:, 2 * T:3 * T], ALU.mult).then_inc(S["gates"], 1)
                dve.wait_ge(S["diffs_exp"], r + 1)
                for l in range(LEVELS):
                    m, n = 2 ** l, level_span(l)
                    zf, zs = halves(HG.Z[:, l * T:l * T + n], m)
                    dve.tensor_tensor(zf, zf, halves(key[:, 0:n], m)[0], ALU.mult)
                    z = dve.tensor_tensor(zs, zs, halves(query[:, 0:n], m)[1], ALU.mult)
                z.then_inc(S["pairs_ready"], 1)
            if tail:
                dve.wait_ge(S["o_hi"], t + 1)
                dve.tensor_tensor(o_lo[:, bass.ds(t, 1), :], on.unsqueeze(1), o_hi[:, bass.ds(t, 1), :].bitcast(F32),
                                  ALU.subtract).then_inc(S["o_done"], 1)

        def hgrn_pe(pe, j, gemm, main, tail):
            r, t = j - 1, j - 2

            def mm(k):
                if gemm:
                    on_position(lambda eng, ph, jj, kk: gemm_chunk(eng, ph, jj, kk, H_HI, H_LO, KT), pe, j, k)
            mm(0); mm(1)
            if main:
                pe.wait_ge(evacuated, tile_number(IN, r, 2) + 1)
                if tail:
                    pe.wait_ge(S["k_tok"], t + 1)
                for n, (b0, bn) in enumerate(BLOCKS):
                    tr = pe.transpose(TR[0:bn, n * P:(n + 1) * P], vfm[:, b0:b0 + bn], ident[:])
                tr.then_inc(S["v_turned"], 1)
            if tail:
                pe.wait_ge(S["k_tok"], t + 1)
                pe.wait_ge(S["att_ready"], t + 1)
            mm(2)
            if tail:
                for n, (b0, bn) in enumerate(BLOCKS):
                    su = pe.matmul(SU[:, n * P:(n + 1) * P], ktok[0:bn, n, :], vtok[0:bn, n, :], start=True, stop=True)
                su.then_inc(S["updates"], 1)
            mm(3)
            if tail:
                pe.wait_ge(S["states"], t + 1)
                for n, (b0, bn) in enumerate(BLOCKS):
                    v = vtok[0:bn, n, :]
                    for l in range(LEVELS if n < 2 else 5):
                        scores = lev[:, n, l * 64:l * 64 + 64] if n < 2 else lev_s[:, l, :]
                        pe.matmul(halves(OV[:, b0:b0 + bn], 2 ** l)[1], v, scores, start=(l == 0), stop=False,
                                  skip_group_check=True)
                    if n > 0:
                        pe.matmul(OV[:, b0:b0 + bn], (s_mid, s_old)[n - 1][:], qb[:, b0:b0 + bn], start=False, stop=False,
                                  skip_group_check=True)
                    ov = pe.matmul(OV[:, b0:b0 + bn], v, diag[0:bn, b0:b0 + bn], start=False, stop=True,
                                   skip_group_check=True)
                ov.then_inc(S["o_raw"], 1)
            mm(4)
            mm(5)
            if tail:
                pe.wait_ge(S["o_squared"], t + 1)
                pe.matmul(GS[:, 0:T], ones[:], o_sq, start=True, stop=True).then_inc(S["o_summed"], 1)
            mm(6)
            if main:
                pe.wait_ge(S["ke_ready"], r + 1)
                pe.wait_ge(S["v_tok"], r + 1)
                for n, (b0, bn) in enumerate(BLOCKS):
                    tr = pe.transpose(TR[0:bn, n * P:(n + 1) * P], ke[:, b0:b0 + bn], ident[:])
                tr.then_inc(S["k_turned"], 1)
            mm(7)
            if main:
                pe.wait_ge(S["pairs_ready"], r + 1)
                if tail:
                    pe.wait_ge(S["o_ready"], t + 1)
                for b0, lv in ((0, LVA), (P, LVB)):
                    for l in range(LEVELS):
                        z = HG.Z[:, l * T + b0:l * T + b0 + P]
                        pe.matmul(lv[:, l * 64:l * 64 + 64], z, halves(z, 2 ** l)[1], start=True, stop=True)
                    pe.matmul(DG[:, b0:b0 + P], key[:, b0:b0 + P], query[:, b0:b0 + P], start=True, stop=True)
                for l in range(5):
                    z = HG.Z[:, l * T + TP:l * T + T]
                    pe.matmul(DG[0:TS, T + l * 16:T + l * 16 + 16], z, halves(z, 2 ** l)[1], start=True, stop=True)
                pe.matmul(DG[0:TS, TP:T], key[:, TP:T], query[:, TP:T], start=True, stop=True)\
                    .then_inc(S["levels_done"], 1)

        def state_load(eng, t):
            eng.dma_start(s_old[:], a["s_in"][bass.ds(t, 1), :, :].rearrange("h k v -> k (h v)")).then_inc(S["s_loaded"], 16)

        def run_hgrn(eng, step):
            step(eng, 0, True, False, False)
            step(eng, 1, True, True, False)
            step(eng, 2, True, True, True)
            with eng.Fori(3, HEADS) as j:
                step(eng, j, True, True, True)
            step(eng, HEADS, False, True, True)
            step(eng, HEADS + 1, False, False, True)

        y_kept, y_squared = sem("y_kept"), sem("y_squared")
        sq = sb("sq", [P, T])
        y_done = sem("y_done")
        y_count = {}
        sq_count = {}
        n_kept = n_sq = 0
        n_done = 4
        for name, trips, _, tiles in order:
            if "out" in name or "down" in name:
                mode = {"hgrn_out": "only", "mla_out": "only", "down": "first", "down_last": "first"}.get(name)
                mode = mode or ("first" if name.endswith("0") else "add")
                y_count[name] = (n_done, n_kept, n_sq, mode)
                n_done += trips * tiles
                n_kept += trips * tiles if mode == "add" else 0
                n_sq += trips * tiles if mode != "first" else 0
        TRIPS = {name: trips for name, trips, _, _ in order}

        def out_act(act, phase, i, t):
            act.wait_ge(chunk_done, last_chunk(phase, i, t))
            n = y_count[phase][0] + t
            act.wait_ge(y_done, i * TILES[phase] + (n - 3))
            act.activation(yt[:, t, :], psum[t][:, 0:T], ACT.Copy).then_inc(evacuated, 1)

        def out_dve(dve, phase, i, t, col):
            done0, kept0, sq0, mode = y_count[phase]
            n = TILES[phase]
            dve.wait_ge(evacuated, tile_number(phase, i, t) + 1)
            ycol = Y[:, bass.ds(col, 1), :]
            if mode == "first":
                dve.tensor_copy(ycol, yt[:, t:t + 1, :]).then_inc(y_done, 1)
                return
            dve.wait_ge(y_done, i * n + (done0 + t))
            if mode == "add":
                dve.tensor_tensor(ycol, ycol, yt[:, t:t + 1, :], ALU.add).then_inc(y_kept, 1)
                dve.wait_ge(y_kept, i * n + (kept0 + t + 1))
                dve.tensor_tensor(sq[:].unsqueeze(1), ycol, ycol, ALU.mult).then_inc(y_squared, 1)
            else:
                dve.tensor_copy(ycol, yt[:, t:t + 1, :])
                dve.tensor_tensor(sq[:], yt[:, t, :], yt[:, t, :], ALU.mult).then_inc(y_squared, 1)
            dve.wait_ge(y_squared, i * n + (sq0 + t + 1))
            dve.tensor_tensor(ssq[:], ssq[:], sq[:], ALU.add).then_inc(y_done, 1)

        def run_out(eng, phase, split, drain):
            trips, n = TRIPS[phase], TILES[phase]

            def trip(i, before):
                for t in range(n):
                    for k in tile_chunks(phase, t):
                        split(eng, phase, i, k)
                    if t > 0 or before:
                        drain(eng, phase, i if t else i - 1, t - 1 if t else n - 1)
            trip(0, False)
            if trips > 2:
                with eng.Fori(1, trips) as i:
                    trip(i, True)
            elif trips == 2:
                trip(1, True)
            drain(eng, phase, trips - 1, n - 1)

        def out_col(phase, i, t):
            return i * TILES[phase] + (t + (2 * 4 if phase == "down_last" else 0))

        def run_out_act(act, phase):
            run_out(act, phase, split_hi, out_act)

        def run_out_dve(dve, phase):
            if y_count[phase][3] != "first":
                dve.memset(ssq[:], 0.0).then_inc(filled_ssq, 1)
                dve.wait_ge(filled_ssq, 1 + [p for p in y_count if y_count[p][3] != "first"].index(phase))
            run_out(dve, phase, split_lo, lambda e, ph, i, t: out_dve(e, ph, i, t, out_col(ph, i, t)))

        filled_ssq = sem("filled_ssq")

        def run_out_pe(pe, phase, hi, lo, kt):
            def trip(i):
                for k in range(len(CHUNKS[phase])):
                    gemm_chunk(pe, phase, i, k, hi, lo, kt)
            if TRIPS[phase] > 2:
                trip(0)
                with pe.Fori(1, TRIPS[phase]) as i:
                    trip(i)
            else:
                for i in range(TRIPS[phase]):
                    trip(i)

        stages = [(None, (0, 0)), ((0, 1), (0, 2)), ((0, 3), (1, 0)), ((1, 1), (1, 2)), ((1, 3), None)]
        n_sum, n_log, n_rstd = sem("n_sum"), sem("n_log"), sem("n_rstd")
        y_scaled, x_ready = sem("y_scaled"), sem("x_ready")
        x_squared, x_summed = sem("x_squared"), sem("x_summed")
        n_scaled, n_hi, h_ready = sem("n_scaled"), sem("n_hi"), sem("h_ready")
        stat = {}
        n = 0
        for s, (post, pre) in enumerate(stages):
            stat[s, "post"] = n
            n += post is not None
            stat[s, "pre"] = n
            n += pre is not None
        SQ = [sq[:], LR]

        def rstd(act, n, bank, out, width):
            act.wait_ge(n_sum, n + 1)
            act.activation(out, bank[:, 0:T], ACT.Ln, scale=1.0 / width, bias=eps[:, 0:1]).then_inc(n_log, 1)
            act.wait_ge(n_log, n + 1)
            act.activation(out, out, ACT.Exp, scale=-0.5).then_inc(n_rstd, 1)

        def norm_act(act, s):
            post, pre = stages[s]
            act.add_instruction(mybir.InstLoadActFuncSet(act_func_set_id=EXP_LN_SET, name=nc.get_next_instruction_name(),
                                                         engine=mybir.EngineType.Activation))
            if post:
                rstd(act, stat[s, "post"], psum[4], RSA, D)
            if pre:
                for k in range(KT):
                    q = KT * s + k
                    if s == 0:
                        act.wait_ge(x_in, 16)
                    else:
                        act.wait_ge(x_ready, KT * (s - 1) + k + 1)
                    if q >= 2:
                        act.wait_ge(x_summed, q - 1)
                    act.activation(SQ[k % 2], X[:, k, :], ACT.Square).then_inc(x_squared, 1)
                rstd(act, stat[s, "pre"], psum[5], RSB, D)
                for k in range(KT):
                    act.wait_ge(n_scaled, KT * s + k + 1)
                    act.activation(H_HI[:, k, :], Y[:, k, :], ACT.Copy).then_inc(n_hi, 1)

        def norm_pe(pe, s):
            post, pre = stages[s]
            if post:
                last = [p for p in y_count][{1: 0, 2: 2, 3: 5, 4: 7}[s]]
                done0 = y_count[last][0] + TRIPS[last] * TILES[last]
                pe.wait_ge(y_done, done0)
                pe.matmul(psum[4][:, 0:T], ones[:], ssq[:], start=True, stop=True).then_inc(n_sum, 1)
            if pre:
                for k in range(KT):
                    pe.wait_ge(x_squared, KT * s + k + 1)
                    mm = pe.matmul(psum[5][:, 0:T], ones[:], SQ[k % 2], start=(k == 0), stop=(k == KT - 1))
                    mm.then_inc(x_summed if k < KT - 1 else n_sum, 1)
                pe.wait_ge(n_sum, stat[s, "pre"] + 1)
                pe.sem_inc(x_summed, 1)

        def norm_dve(dve, s):
            post, pre = stages[s]
            if post:
                la, wa = post
                dve.wait_ge(n_rstd, stat[s, "post"] + 1)
                for k in range(KT):
                    dve.scalar_tensor_tensor(out=Y[:, k, :], in0=Y[:, k, :], scalar=norm_w[:, la, wa, k:k + 1], in1=RSA,
                                             op0=ALU.mult, op1=ALU.mult).then_inc(y_scaled, 1)
                for k in range(KT):
                    dve.wait_ge(y_scaled, KT * (s - 1) + k + 1)
                    dve.tensor_tensor(X[:, k, :], X[:, k, :], Y[:, k, :], ALU.add).then_inc(x_ready, 1)
            if pre:
                lb_, wb = pre
                dve.wait_ge(n_rstd, stat[s, "pre"] + 1)
                if s == 0:
                    dve.wait_ge(x_in, 16)
                for k in range(KT + 2):
                    if k < KT:
                        dve.scalar_tensor_tensor(out=Y[:, k, :], in0=X[:, k, :], scalar=norm_w[:, lb_, wb, k:k + 1],
                                                 in1=RSB, op0=ALU.mult, op1=ALU.mult).then_inc(n_scaled, 1)
                    if k >= 2:
                        dve.wait_ge(n_hi, KT * s + k - 1)
                        dve.tensor_tensor(H_LO[:, k - 2, :], Y[:, k - 2, :], H_HI[:, k - 2, :].bitcast(F32),
                                          ALU.subtract).then_inc(h_ready, 1)

        rows_done, conv_step, conv_done = sem("f_rows"), sem("f_conv_step"), sem("f_conv")
        silu_done, prod_done, g_hi_done, g_done = sem("f_silu"), sem("f_prod"), sem("f_g_hi"), sem("f_g")
        conv_stored = sem("conv_stored")
        NI = HF // 2

        def ffn_base(layer, half):
            return 2 * layer + half

        def f_tile(layer, half, i, t):
            return i * 4 + (ffn_base(layer, half) * NI * 4 + t)

        def f_hid(layer, half, i, jj):
            return i * 2 + (ffn_base(layer, half) * NI * 2 + jj)

        def f_col(half, i, t):
            return i * 4 + (half * NI * 4 + t)

        def ffn_act(act, layer, half, i, gemm, prev):
            phase = f"ffn_in{layer}{half}"

            def hi(t):
                if gemm:
                    for k in tile_chunks(phase, t):
                        split_hi(act, phase, i, k)

            def evac(i, t):
                act.wait_ge(chunk_done, last_chunk(phase, i, t))
                act.wait_ge(conv_done, f_tile(layer, half, i, t) + 1)
                act.activation(ext[:, t, 2:2 + TP], psum[t][:, 0:TP], ACT.Copy)
                act.activation(ext[:, t, 4 + TP:EXT], psum[t][:, TP:T], ACT.Copy).then_inc(evacuated, 1)

            def silu(i, jj):
                act.wait_ge(conv_done, f_tile(layer, half, i, 2 * jj) + 5)
                act.activation(cv[:, 2 * jj, :], cv[:, 2 * jj, :], ACT.Silu).then_inc(silu_done, 1)

            def g_top(i, jj):
                act.wait_ge(prod_done, f_hid(layer, half, i, jj) + 1)
                act.activation(g_hi[:, bass.ds(i * 2 + jj, 1), :], prod[:, jj:jj + 1, :], ACT.Copy).then_inc(g_hi_done, 1)

            hi(0)
            if prev:
                g_top(i - 1, 0)
                evac(i - 1, 2)
            hi(1)
            if prev:
                evac(i - 1, 3)
                silu(i - 1, 1)
            hi(2)
            if prev:
                g_top(i - 1, 1)
            if gemm:
                evac(i, 0)
                hi(3)
                evac(i, 1)
                silu(i, 0)

        def ffn_dve(dve, layer, half, i, gemm, prev):
            phase = f"ffn_in{layer}{half}"

            def lo(t):
                if gemm:
                    for k in tile_chunks(phase, t):
                        split_lo(dve, phase, i, k)

            def conv(i, t):
                n = f_tile(layer, half, i, t)
                w = conv_w[:, layer, :, :].rearrange("p c w -> p (c w)")

                def tap(x):
                    return w[:, bass.ds(f_col(half, i, t) * 4 + x, 1)]
                dve.wait_ge(rows_done, n + 1)
                if not (isinstance(i, int) and i == 0 and ffn_base(layer, half) == 0):
                    dve.wait_ge(prod_done, f_hid(layer, half, i, t // 2))
                dve.tensor_scalar(cv[:, t, :], ext[:, t, 2:EXT], tap(2), tap(3), ALU.mult, ALU.add).then_inc(conv_step, 1)
                dve.wait_ge(conv_step, n * 2 + 1)
                dve.scalar_tensor_tensor(out=cv[:, t, :], in0=ext[:, t, 1:EXT - 1], scalar=tap(1), in1=cv[:, t, :],
                                         op0=ALU.mult, op1=ALU.add).then_inc(conv_step, 1)
                dve.wait_ge(conv_step, n * 2 + 2)
                dve.scalar_tensor_tensor(out=cv[:, t, :], in0=ext[:, t, 0:EXT - 2], scalar=tap(0), in1=cv[:, t, :],
                                         op0=ALU.mult, op1=ALU.add).then_inc(conv_done, 1)

            def gated(i, jj):
                dve.wait_ge(silu_done, f_hid(layer, half, i, jj) + 1)
                dve.wait_ge(conv_done, f_tile(layer, half, i, 2 * jj + 1) + 5)
                dve.tensor_tensor(prod[:, jj, 0:TP], cv[:, 2 * jj, 0:TP], cv[:, 2 * jj + 1, 0:TP], ALU.mult)
                dve.tensor_tensor(prod[:, jj, TP:T], cv[:, 2 * jj, TP + 2:T + 2], cv[:, 2 * jj + 1, TP + 2:T + 2],
                                  ALU.mult).then_inc(prod_done, 1)

            def g_rest(i, jj):
                dve.wait_ge(g_hi_done, f_hid(layer, half, i, jj) + 1)
                at = bass.ds(i * 2 + jj, 1)
                dve.tensor_tensor(g_lo[:, at, :], prod[:, jj:jj + 1, :], g_hi[:, at, :].bitcast(F32),
                                  ALU.subtract).then_inc(g_done, 1)

            lo(0)
            if prev:
                g_rest(i - 1, 0)
                conv(i - 1, 2)
            lo(1)
            if prev:
                conv(i - 1, 3)
                gated(i - 1, 1)
            lo(2)
            if gemm:
                conv(i, 0)
            if prev:
                g_rest(i - 1, 1)
            if gemm:
                lo(3)
                conv(i, 1)
                gated(i, 0)

        def ffn_pool(pool, layer, half, i):
            for t in range(4):
                pool.wait_ge(evacuated, tile_number(f"ffn_in{layer}{half}", i, t) + 1)
                at = bass.ds(f_col(half, i, t), 1)
                pool.tensor_copy(ext[:, t:t + 1, 2 + TP:4 + TP], conv_old[:, layer, at, :])
                new = ext[:, t, EXT - 2 * (TS + 2):EXT].rearrange("p (s c) -> p s c", c=TS + 2)[:, :, TS:TS + 2]
                pool.tensor_copy(conv_new[:, at, :].rearrange("p a (s c) -> p (a s) c", c=2), new).then_inc(rows_done, 1)

        def run_ffn_in(eng, step, layer, half):
            step(eng, layer, half, 0, True, False)
            with eng.Fori(1, NI) as i:
                step(eng, layer, half, i, True, True)
            step(eng, layer, half, NI, False, True)

        CQ_HI = h_hi[:, 0:LATENT * T].rearrange("p (k t) -> p k t", t=T)
        CQ_LO = h_lo[:, 0:LATENT * T].rearrange("p (k t) -> p k t", t=T)
        CK_HI = h_hi[:, LATENT * T:LATENT * (T + TK)].rearrange("p (k t) -> p k t", t=TK)
        CK_LO = h_lo[:, LATENT * T:LATENT * (T + TK)].rearrange("p (k t) -> p k t", t=TK)
        cache = Y[:, 9:12, :].rearrange("p k t -> p (k t)")[:, 0:LATENT * PAST].rearrange("p (k t) -> p k t", t=PAST)
        kpe = Y[:, 12:14, :].rearrange("p k t -> p (k t)")[:, 0:TK]
        m = {n: sem("m_" + n) for n in [
            "cache_in", "squared", "summed", "scaled", "hi", "latents", "swapped_k", "kpe_parts", "kpe_ready", "out_dma",
            "swapped", "rope_parts", "q_ready", "scores", "masked", "maxes", "bounds", "probs", "recips", "normed",
            "v_turned", "v_tok", "p_turned", "p_tok", "o_raw", "o_hi", "o_done"]}
        qn = [qraw[:], graw[:]]
        qp = vfm[:]
        kn = [lev[:, n, 0:TK] for n in range(2)]
        values = row_tiles[:, 7:10, :].rearrange("p k t -> p (k t)")
        vf = [values[:, n * TK:(n + 1) * TK] for n in range(2)]
        qr = [key[:], query[:]]
        r1, r2 = gate[:], fgate[:]
        vt = [g_f32 for g_f32 in (Y[:, 0:2, :].rearrange("p k t -> p (k t)")[:, 0:4 * P],
                                  Y[:, 2:4, :].rearrange("p k t -> p (k t)")[:, 0:4 * P])]
        PR = TP + P + PAST + TS
        pr = [Y[:, 4:6, :].rearrange("p k t -> p (k t)")[:, 0:PR], Y[:, 6:8, :].rearrange("p k t -> p (k t)")[:, 0:PR]]
        pt = [ktok[:].rearrange("p a b -> p (a b)"), vtok[:].rearrange("p a b -> p (a b)")]
        pt_s = [s_new[:, 0, 0:2 * TS], s_new[:, 1, 0:2 * TS]]
        mx = sb("mx", [P, 2, 3])
        nb = sb("nb", [P, 2, 3])
        sums = sb("sums", [P, 2, 3])
        rc = sb("rc", [P, 2, 3])
        SC = [psum[5], psum[7]]
        SS = psum[6]
        SPANS = [(0, P), (P, TP)]
        PAIR = "pairs"

        def latent_act(act):
            act.add_instruction(mybir.InstLoadActFuncSet(act_func_set_id=EXP_LN_SET, name=nc.get_next_instruction_name(),
                                                         engine=mybir.EngineType.Activation))
            done = y_count["down_last"][0] + 1
            act.wait_ge(y_done, done)
            for k in range(2 * LATENT):
                if k >= 2:
                    act.wait_ge(m["summed"], k - 1)
                act.activation(SQ[k % 2], Y[:, k, :], ACT.Square).then_inc(m["squared"], 1)
            for n, out in ((0, RSA), (1, RSB)):
                act.wait_ge(m["summed"], 2 * LATENT)
                act.activation(out, psum[4 + n][:, 0:T], ACT.Ln, scale=1.0 / (LATENT * P),
                               bias=eps[:, 0:1]).then_inc(m["scaled"], 1)
                act.wait_ge(m["scaled"], 2 * n + 1)
                act.activation(out, out, ACT.Exp, scale=-0.5).then_inc(m["scaled"], 1)
            act.wait_ge(m["cache_in"], 16 * (LATENT + 2))
            act.activation(CK_HI[:, :, TP:TP + PAST], cache, ACT.Copy).then_inc(m["hi"], 1)
            for k in range(2 * LATENT):
                act.wait_ge(m["scaled"], 4 + k + 1)
                if k < LATENT:
                    act.activation(CQ_HI[:, k, :], Y[:, k, :], ACT.Copy).then_inc(m["hi"], 1)
                else:
                    act.activation(CK_HI[:, k - LATENT, 0:TP], Y[:, k, 0:TP], ACT.Copy)
                    act.activation(CK_HI[:, k - LATENT, TP + PAST:TK], Y[:, k, TP:T], ACT.Copy).then_inc(m["hi"], 1)

        def latent_pe(pe):
            for k in range(2 * LATENT):
                n = k // LATENT
                pe.wait_ge(m["squared"], k + 1)
                pe.matmul(psum[4 + n][:, 0:T], ones[:], SQ[k % 2], start=(k % LATENT == 0),
                          stop=(k % LATENT == LATENT - 1)).then_inc(m["summed"], 1)
            pe.wait_ge(y_done, y_count["down_last"][0] + 1)
            pe.matmul(psum[6][:, 0:T], swap[:], Y[:, 2 * LATENT, :], start=True, stop=True).then_inc(m["swapped_k"], 1)

        def latent_dve(dve):
            for n in range(2):
                dve.memset(qr[n], 0.0)
            dve.memset(mx[:], 0.0)
            dve.memset(sums[:], 1.0).then_inc(filled, 1)
            dve.wait_ge(m["scaled"], 4)
            for k in range(2 * LATENT):
                dve.scalar_tensor_tensor(out=Y[:, k, :], in0=Y[:, k, :], scalar=lat_w[:, k // LATENT, k % LATENT:k % LATENT + 1],
                                         in1=RSA if k < LATENT else RSB, op0=ALU.mult, op1=ALU.mult).then_inc(m["scaled"], 1)
            dve.wait_ge(m["hi"], 1)
            dve.tensor_tensor(CK_LO[:, :, TP:TP + PAST], cache, CK_HI[:, :, TP:TP + PAST].bitcast(F32), ALU.subtract)
            for k in range(2 * LATENT):
                dve.wait_ge(m["hi"], k + 2)
                if k < LATENT:
                    dve.tensor_tensor(CQ_LO[:, k, :], Y[:, k, :], CQ_HI[:, k, :].bitcast(F32), ALU.subtract)
                else:
                    kk = k - LATENT
                    dve.tensor_tensor(CK_LO[:, kk, 0:TP], Y[:, k, 0:TP], CK_HI[:, kk, 0:TP].bitcast(F32), ALU.subtract)
                    z = dve.tensor_tensor(CK_LO[:, kk, TP + PAST:TK], Y[:, k, TP:T], CK_HI[:, kk, TP + PAST:TK].bitcast(F32),
                                          ALU.subtract)
            z.then_inc(m["latents"], 1)
            dve.wait_ge(m["swapped_k"], 1)
            dve.tensor_tensor(r1, Y[:, 2 * LATENT, :], cos[:], ALU.mult)
            dve.tensor_tensor(r2, psum[6][:, 0:T], sin[:], ALU.mult).then_inc(m["kpe_parts"], 1)
            dve.wait_ge(m["kpe_parts"], 1)
            dve.tensor_tensor(kpe[:, 0:TP], r1[:, 0:TP], r2[:, 0:TP], ALU.add)
            dve.tensor_tensor(kpe[:, TP + PAST:TK], r1[:, TP:T], r2[:, TP:T], ALU.add).then_inc(m["kpe_ready"], 1)

        def pair_gemm(pe, j, k):
            ch = Chunk(PAIR, j, k)
            pe.wait_ge(lo_done, ch.number + 1)
            tiles = {0: [0, 1], 1: [2], 2: [3, 4], 3: [5, 6]}[k]
            for n, t in enumerate(tiles):
                if not (isinstance(j, int) and j == 0 and t < 4):
                    pe.wait_ge(evacuated, tile_number(PAIR, j, t) - 2)
                if t in (2, 3) and not (isinstance(j, int) and j == 0):
                    pe.wait_ge(m["v_tok"], 2 * j)
                width, hi, lo = (T, CQ_HI, CQ_LO) if t < 3 else (TK, CK_HI, CK_LO)
                for u in range(LATENT):
                    mm = product(pe, psum[t % 4][:, 0:width], ch, n * LATENT + u, hi[:, u, :], lo[:, u, :],
                                 u == 0, u == LATENT - 1)
            mm.then_inc(chunk_done, 1)

        def pair_evac(act, j, ts):
            dst = {0: qn[0], 1: qn[1], 2: qp, 3: kn[0], 4: kn[1], 5: vf[0], 6: vf[1]}
            for t in ts:
                act.wait_ge(chunk_done, Chunk(PAIR, j, {0: 0, 1: 0, 2: 1, 3: 2, 4: 2, 5: 3, 6: 3}[t]).number + 1)
                act.activation(dst[t], psum[t % 4][:, 0:T if t < 3 else TK], ACT.Copy).then_inc(evacuated, 1)

        def pair_act(act, j, gemm, attn, ahead):
            r = j - 1

            def turned_probs(n):
                if attn:
                    act.wait_ge(m["p_turned"], 2 * r + n + 1)
                    act.activation(pt[n], SC[n][:, 0:3 * P], ACT.Copy)
                    act.activation(pt_s[n][:, 0:TS], SC[n][:, 3 * P:3 * P + TS], ACT.Copy)
                    act.activation(pt_s[n][0:TS, TS:2 * TS], SC[n][0:TS, 3 * P + TS:3 * P + 2 * TS], ACT.Copy)\
                        .then_inc(m["p_tok"], 1)

            def out_hi(n):
                if attn:
                    act.wait_ge(m["o_raw"], 2 * r + n + 1)
                    act.activation(o_hi[:, bass.ds(2 * r + n, 1), :], (psum[6], psum[4])[n][:, 0:T].unsqueeze(1), ACT.Copy)\
                        .then_inc(m["o_hi"], 1)

            if attn:
                for n in range(2):
                    act.wait_ge(m["v_turned"], 2 * r + n + 1)
                    bank = psum[3 - n]
                    act.activation(vt[n][:, 0:3 * P], bank[:, 0:3 * P], ACT.Copy)
                    act.activation(vt[n][0:TS, 3 * P:4 * P], bank[0:TS, 3 * P:4 * P], ACT.Copy).then_inc(m["v_tok"], 1)
                for n in range(2):
                    act.wait_ge(m["bounds"], 2 * r + n + 1)
                    for tile, (c0, cn) in enumerate(SPANS):
                        act.activation(pr[n][:, c0:c0 + cn], pr[n][:, c0:c0 + cn], ACT.Exp, bias=nb[:, n, tile:tile + 1],
                                       scale=SCALE, accum_out=sums[:, n, tile:tile + 1])
                for n in range(2):
                    act.activation(pr[n][0:TS, 3 * P:PR], SS[0:TS, n * 160:n * 160 + 160], ACT.Exp, bias=nb[0:TS, n, 2:3],
                                   scale=SCALE, accum_out=sums[0:TS, n, 2:3]).then_inc(m["probs"], 1)
            for k, tiles in enumerate(([0, 1], [2], [3, 4], [5, 6])):
                if k == 1:
                    turned_probs(0)
                if k == 2:
                    turned_probs(1)
                    out_hi(0)
                if k == 3:
                    out_hi(1)
                if gemm:
                    pair_evac(act, j, tiles)
                if ahead:
                    split_hi(act, PAIR, j + 1, k)

        def pair_dve(dve, j, gemm, attn, ahead):
            r = j - 1
            if attn:
                dve.wait_ge(m["scores"], 2 * r + 2)
                for n in range(2):
                    dve.tensor_tensor(pr[n][:, 0:3 * P], SC[n][:, 0:3 * P], chunk_mask[:], ALU.add).then_inc(m["masked"], 1)
                    dve.tensor_reduce(mx[0:TS, n, 2:3], SS[0:TS, n * 160:n * 160 + 160], AX_X, ALU.max)
                    dve.wait_ge(m["masked"], 2 * r + n + 1)
                    for tile, (c0, cn) in enumerate(SPANS):
                        z = dve.tensor_reduce(mx[:, n, tile:tile + 1], pr[n][:, c0:c0 + cn], AX_X, ALU.max)
                    z.then_inc(m["maxes"], 1)
                    dve.wait_ge(m["maxes"], 2 * r + n + 1)
                    dve.tensor_scalar(nb[:, n, :], mx[:, n, :], -SCALE, None, ALU.mult).then_inc(m["bounds"], 1)
                for n in range(2):
                    dve.wait_ge(m["probs"], 2 * r + n + 1)
                    dve.reciprocal(rc[:, n, :], sums[:, n, :]).then_inc(m["recips"], 1)
                    dve.wait_ge(m["recips"], 2 * r + n + 1)
                    for tile, (c0, cn) in enumerate(SPANS):
                        dve.tensor_scalar(pr[n][:, c0:c0 + cn], pr[n][:, c0:c0 + cn], rc[:, n, tile:tile + 1], None, ALU.mult)
                    dve.tensor_scalar(pr[n][0:TS, 3 * P:PR], pr[n][0:TS, 3 * P:PR], rc[0:TS, n, 2:3], None, ALU.mult)\
                        .then_inc(m["normed"], 1)
            for k in range(4):
                if k == 2 and attn:
                    for n, bank in enumerate((psum[6], psum[4])):
                        dve.wait_ge(m["o_hi"], 2 * r + n + 1)
                        at = bass.ds(2 * r + n, 1)
                        dve.tensor_tensor(o_lo[:, at, :], bank[:, 0:T].unsqueeze(1), o_hi[:, at, :].bitcast(F32),
                                          ALU.subtract).then_inc(m["o_done"], 1)
                if k == 2 and gemm:
                    dve.wait_ge(m["swapped"], j + 1)
                    dve.tensor_tensor(r1, qp, cos[:], ALU.mult)
                    dve.tensor_tensor(r2, psum[4][:, 0:T], sin[:], ALU.mult).then_inc(m["rope_parts"], 1)
                    dve.wait_ge(m["rope_parts"], j + 1)
                    for n in range(2):
                        h = slice(64 * n, 64 * n + 64)
                        z = dve.tensor_tensor(qr[n][h, :], r1[h, :], r2[h, :], ALU.add)
                    z.then_inc(m["q_ready"], 1)
                if ahead:
                    split_lo(dve, PAIR, j + 1, k)

        def pair_pe(pe, j, gemm, attn, ahead):
            r = j - 1

            def turn(n):
                if attn:
                    pe.wait_ge(m["normed"], 2 * r + n + 1)
                    bank = SC[n]
                    for c in range(3):
                        pe.transpose(bank[:, c * P:(c + 1) * P], pr[n][:, c * P:(c + 1) * P], ident[:])
                    pe.transpose(bank[:, 3 * P:3 * P + TS], pr[n][0:TS, 3 * P:4 * P], ident[0:TS, 0:TS])
                    pe.transpose(bank[0:TS, 3 * P + TS:3 * P + 2 * TS], pr[n][0:TS, 4 * P:PR], ident[0:TS, 0:TS])\
                        .then_inc(m["p_turned"], 1)

            def outputs(n):
                if attn:
                    pe.wait_ge(m["p_tok"], 2 * r + n + 1)
                    pe.wait_ge(m["v_tok"], 2 * r + 2)
                    bank = (psum[6], psum[4])[n]
                    v = [vt[n][:, c * P:(c + 1) * P] for c in range(3)]
                    pe.matmul(bank[:, 0:P], v[0], pt[n][:, 0:P], start=True, stop=True)
                    pe.matmul(bank[:, P:TP], v[0], pt[n][:, P:2 * P], start=True, stop=False)
                    pe.matmul(bank[:, P:TP], v[1], pt[n][:, 2 * P:3 * P], start=False, stop=True)
                    pe.matmul(bank[:, TP:T], v[2], pt_s[n][:, 0:TS], start=True, stop=False)
                    pe.matmul(bank[:, TP:T], vt[n][0:TS, 3 * P:4 * P], pt_s[n][0:TS, TS:2 * TS], start=False,
                              stop=True).then_inc(m["o_raw"], 1)

            if gemm:
                pair_gemm(pe, j, 0)
            turn(0)
            if gemm:
                pair_gemm(pe, j, 1)
            turn(1)
            outputs(0)
            if gemm:
                pair_gemm(pe, j, 2)
            outputs(1)
            if gemm:
                if attn:
                    pe.wait_ge(m["o_done"], 2 * r + 2)
                pe.wait_ge(evacuated, tile_number(PAIR, j, 2) + 1)
                pe.matmul(psum[4][:, 0:T], swap[:], qp, start=True, stop=True).then_inc(m["swapped"], 1)
                pair_gemm(pe, j, 3)
                pe.wait_ge(m["q_ready"], j + 1)
                pe.wait_ge(evacuated, tile_number(PAIR, j, 4) + 1)
                for n in range(2):
                    for c0, q0, k0, kn_ in ((0, 0, 0, P), (P, P, 0, TP)):
                        out = SC[n][:, c0:c0 + kn_]
                        pe.matmul(out, qn[n][:, q0:q0 + P], kn[n][:, k0:k0 + kn_], start=True, stop=False)
                        pe.matmul(out, qr[n][:, q0:q0 + P], kpe[:, k0:k0 + kn_], start=False, stop=True)
                    out = SS[0:TS, n * 160:n * 160 + 160]
                    pe.matmul(out, qn[n][:, TP:T], kn[n][:, TP:TK], start=True, stop=False)
                    pe.matmul(out, qr[n][:, TP:T], kpe[:, TP:TK], start=False, stop=True).then_inc(m["scores"], 1)
                for n in range(2):
                    pe.wait_ge(evacuated, tile_number(PAIR, j, 5 + n) + 1)
                    bank = psum[3 - n]
                    for c in range(4):
                        w = P if c < 3 else TS
                        tr = pe.transpose(bank[0:w, c * P:(c + 1) * P], vf[n][:, c * P:c * P + w], ident[:])
                    tr.then_inc(m["v_turned"], 1)

        def run_pairs(eng, split, step):
            if split:
                for k in range(4):
                    split(eng, PAIR, 0, k)
            step(eng, 0, True, False, True)
            with eng.Fori(1, PAIRS - 1) as j:
                step(eng, j, True, True, True)
            step(eng, PAIRS - 1, True, True, False)
            step(eng, PAIRS, False, True, False)

        y_out = sem("y_out")
        block = ctx.enter_context(nc.Block())

        @block.sync
        def _(sp):
            sp.dma_start(X[:], a["x"]).then_inc(x_in, 16)
            for k in range(len(CHUNKS[IN])):
                ch = CHUNKS[IN][k]
                ring_load(sp, a["w_hi_in"], IN, 0, k, ch[0])
            with sp.Fori(1, HEADS) as i:
                for k in range(len(CHUNKS[IN])):
                    ring_load(sp, a["w_hi_in"], IN, i, k, i * 4 + CHUNKS[IN][k][0])

            def load(w, phase, first):
                with sp.Fori(0, TRIPS[phase]) as i:
                    for k in range(len(CHUNKS[phase])):
                        ring_load(sp, w, phase, i, k, i * TILES[phase] + (first + CHUNKS[phase][k][0]))
            load(a["w_ho"], "hgrn_out", 0)
            for layer in range(2):
                if layer == 1:
                    load(a["w_down"], "down", 0)
                    for k in range(len(CHUNKS["down_last"])):
                        ring_load(sp, a["w_down"], "down_last", 0, k, 8)
                    with sp.Fori(0, PAIRS) as i:
                        for k in range(4):
                            ring_load(sp, a["w_uq"] if k < 2 else a["w_ukv"], PAIR, i, k, i)
                    load(a["w_mo"], "mla_out", 0)
                for half in range(2):
                    load(a["w_fi"], f"ffn_in{layer}{half}", (2 * layer + half) * 2 * HF)
                    load(a["w_fo"], f"ffn_out{layer}{half}", (2 * layer + half) * KT)
            sp.wait_ge(S["s_stored"], 32 * HEADS)
            for k in range(KT):
                sp.wait_ge(x_ready, KT * 3 + k + 1)
                sp.dma_start(a["o_y"][:, k, :], X[:, k, :]).then_inc(y_out, 16)
            sp.wait_ge(y_out, 16 * KT)

        @block.gpsimd
        def _(pool):
            loads = [(norm_w[:], a["norm_w"]), (lbl[:], a["lbl"]), (gnorm_w[:], a["gnorm_w"]), (ident[:], a["ident"]),
                     (carry[:], a["carry"]), (level_mask_f[:], a["level_mask"]),
                     (conv_w[:], a["conv_w"]), (conv_old[:], a["conv_old"]), (lat_w[:], a["lat_w"]), (swap[:], a["swap"]),
                     (cos[:], a["cos"]), (sin[:], a["sin"]), (chunk_mask[:], a["chunk_mask"])]
            for dst, src in loads:
                pool.dma_start(dst, src).then_inc(consts_in, 16)
            pool.wait_ge(consts_in, 16 * len(loads))
            for layer in range(2):
                if layer == 1:
                    pool.wait_ge(h_ready, 3 * KT)
                    pool.dma_start(cache, a["cache"]).then_inc(m["cache_in"], 16 * LATENT)
                    for n in range(2):
                        pool.dma_start(kpe[64 * n:64 * n + 64, TP:TP + PAST], a["cache_kpe"]).then_inc(m["cache_in"], 16)
                    pool.wait_ge(m["scaled"], 4 + 2 * LATENT)
                    pool.dma_start(a["o_ckv"], Y[:, LATENT:2 * LATENT, :]).then_inc(m["out_dma"], 16)
                    pool.wait_ge(m["kpe_ready"], 1)
                    pool.dma_start(a["o_kpe"][:, 0:TP], kpe[0:64, 0:TP]).then_inc(m["out_dma"], 16)
                    pool.dma_start(a["o_kpe"][:, TP:T], kpe[0:64, TP + PAST:TK]).then_inc(m["out_dma"], 16)
                    pool.wait_ge(m["out_dma"], 48)
                    pool.wait_ge(conv_stored, 16)
                for half in range(2):
                    with pool.Fori(0, NI) as i:
                        ffn_pool(pool, layer, half, i)
                pool.wait_ge(rows_done, (layer + 1) * NI * 8)
                pool.dma_start(a["o_conv"][layer], conv_new[:]).then_inc(conv_stored, 16)
            pool.wait_ge(conv_stored, 32)

        @block.scalar
        def _(act):
            act.wait_ge(filled, 1)
            state_load(act, 0)
            norm_act(act, 0)
            act.wait_ge(S["lb_ready"], 1)
            act.activation(lbt[:, 0:3, :], lbt[:, 0:3, :], ACT.Exp).then_inc(S["lb_ready"], 1)
            run_hgrn(act, hgrn_act)
            run_out_act(act, "hgrn_out")
            norm_act(act, 1)
            for layer in range(2):
                if layer == 1:
                    run_out_act(act, "down")
                    run_out_act(act, "down_last")
                    latent_act(act)
                    act.wait_ge(m["latents"], 1)
                    run_pairs(act, split_hi, pair_act)
                    run_out_act(act, "mla_out")
                    norm_act(act, 3)
                for half in range(2):
                    act.add_instruction(mybir.InstLoadActFuncSet(act_func_set_id=SILU_SET, name=nc.get_next_instruction_name(),
                                                                 engine=mybir.EngineType.Activation))
                    run_ffn_in(act, ffn_act, layer, half)
                    run_out_act(act, f"ffn_out{layer}{half}")
                norm_act(act, 2 if layer == 0 else 4)

        @block.vector
        def _(dve):
            dve.memset(ones[:], 1.0).then_inc(y_done, 4)
            dve.memset(eps[:], EPS).then_inc(filled, 1)
            dve.wait_ge(consts_in, 16 * 13)
            steps = sem("lb_steps")
            dve.tensor_tensor(lbt[:, 3, :], lbl[:, 0, :], lbl[:, 1, :], ALU.max).then_inc(steps, 1)
            dve.wait_ge(steps, 1)
            dve.tensor_tensor(lbt[:, 3, :], lbt[:, 3, :], lbl[:, 2, :], ALU.max).then_inc(steps, 1)
            dve.wait_ge(steps, 2)
            for n in range(3):
                z = dve.tensor_tensor(lbt[:, n, :], lbl[:, n, :], lbt[:, 3, :], ALU.subtract)
            z.then_inc(S["lb_ready"], 1)
            norm_dve(dve, 0)
            dve.wait_ge(S["lb_ready"], 2)
            dve.tensor_tensor(lbt[:, 1, :], lbt[:, 1, :], lbt[:, 2, :], ALU.add).then_inc(steps, 1)
            dve.wait_ge(steps, 3)
            dve.tensor_tensor(lbt[:, 3, :], lbt[:, 0, :], lbt[:, 1, :], ALU.add).then_inc(steps, 1)
            dve.wait_ge(steps, 4)
            dve.reciprocal(lbt[:, 3, :], lbt[:, 3, :]).then_inc(steps, 1)
            dve.wait_ge(steps, 5)
            dve.tensor_tensor(lb[:], lbt[:, 0, :], lbt[:, 3, :], ALU.mult)
            dve.tensor_tensor(oml[:], lbt[:, 1, :], lbt[:, 3, :], ALU.mult).then_inc(steps, 1)
            dve.wait_ge(steps, 6)
            run_hgrn(dve, hgrn_dve)
            run_out_dve(dve, "hgrn_out")
            dve.wait_ge(S["s_stored"], 32 * HEADS)
            dve.memset(ext[:, :, 0:2], 0.0).then_inc(conv_done, 4)
            norm_dve(dve, 1)
            for layer in range(2):
                if layer == 1:
                    run_out_dve(dve, "down")
                    run_out_dve(dve, "down_last")
                    latent_dve(dve)
                    dve.wait_ge(m["out_dma"], 48)
                    run_pairs(dve, split_lo, pair_dve)
                    run_out_dve(dve, "mla_out")
                    norm_dve(dve, 3)
                    dve.memset(ext[:, :, 0:2], 0.0)
                for half in range(2):
                    run_ffn_in(dve, ffn_dve, layer, half)
                    run_out_dve(dve, f"ffn_out{layer}{half}")
                norm_dve(dve, 2 if layer == 0 else 4)

        @block.tensor
        def _(pe):
            pe.wait_ge(filled, 1)
            pe.wait_ge(consts_in, 16 * 13)
            norm_pe(pe, 0)
            pe.wait_ge(h_ready, KT)
            run_hgrn(pe, hgrn_pe)
            pe.wait_ge(S["o_done"], HEADS)
            run_out_pe(pe, "hgrn_out", o_hi, o_lo, KT)
            norm_pe(pe, 1)
            pe.wait_ge(h_ready, 2 * KT)
            for layer in range(2):
                if layer == 1:
                    run_out_pe(pe, "down", H_HI, H_LO, KT)
                    run_out_pe(pe, "down_last", H_HI, H_LO, KT)
                    latent_pe(pe)
                    pe.wait_ge(m["latents"], 1)
                    pe.wait_ge(m["kpe_ready"], 1)
                    pe.wait_ge(m["cache_in"], 16 * (LATENT + 2))
                    run_pairs(pe, None, pair_pe)
                    pe.wait_ge(m["o_done"], HEADS)
                    run_out_pe(pe, "mla_out", o_hi, o_lo, KT)
                    norm_pe(pe, 3)
                    pe.wait_ge(h_ready, 4 * KT)
                for half in range(2):
                    run_out_pe(pe, f"ffn_in{layer}{half}", H_HI, H_LO, KT)
                    pe.wait_ge(g_done, (ffn_base(layer, half) + 1) * HF)
                    run_out_pe(pe, f"ffn_out{layer}{half}", g_hi, g_lo, HF)
                norm_pe(pe, 2 if layer == 0 else 4)
                if layer == 0:
                    pe.wait_ge(h_ready, 3 * KT)


def kernel(x_prompt, x_sample, state_hgrn, cache_ckv, cache_kpe, state_conv, norm_w, lb_logits, hgrn_w_in, hgrn_gnorm_w,
           hgrn_w_out, mla_w_down, mla_q_norm_w, mla_kv_norm_w, mla_w_uq, mla_w_ukv, mla_w_out, ffn_w_in, ffn_conv_w,
           ffn_conv_b, ffn_w_out):
    import numpy as np
    import concourse.bacc as _bacc
    from concourse.bass_utils import run_bass_kernel_spmd as _run

    f = lambda v: np.asarray(v)
    D = x_prompt.shape[-1]
    KT = D // P
    H = D // P
    FF = ffn_w_out.shape[1]
    FT = FF // P
    HF = FT // 2
    lora = LATENT * P

    def rows(w):
        return w.reshape(-1, P, w.shape[-1]).transpose(1, 0, 2)

    def tiles(w, kt=None):
        k, n = w.shape
        return w.reshape(k // P, P, n // P, P).transpose(2, 1, 0, 3).reshape(n // P, P, k)

    A = {}
    A["x"] = rows(np.concatenate([f(x_prompt)[0], f(x_sample)[0]], 0).T)
    A["s_in"] = f(state_hgrn)[0, 0]
    A["norm_w"] = f(norm_w).reshape(2, 4, KT, P).transpose(3, 0, 1, 2)
    A["lbl"] = f(lb_logits).reshape(3, KT, P).transpose(2, 0, 1)
    A["gnorm_w"] = f(hgrn_gnorm_w)[0][:, None]
    w = tiles(f(hgrn_w_in)[0]).reshape(4, H, P, D)
    A["w_hi_in"] = w[[1, 0, 2, 3]].transpose(1, 0, 2, 3).reshape(4 * H, P, D)
    A["w_ho"] = tiles(f(hgrn_w_out)[0])
    w = f(mla_w_down)[0]
    A["w_down"] = tiles(np.concatenate([w, w[:, 2 * lora:]], 1))
    uq = f(mla_w_uq)[0].reshape(lora, H, 192)
    nope = tiles(uq[:, :, :128].reshape(lora, H * P)).reshape(H // 2, 2, P, lora)
    pe_ = tiles(uq[:, :, 128:].reshape(lora, H * 64)).reshape(H // 2, 1, P, lora)
    A["w_uq"] = np.concatenate([nope, pe_], 1).transpose(0, 2, 1, 3).reshape(H // 2, P, 3 * lora)
    ukv = f(mla_w_ukv)[0].reshape(lora, H, 2, P)
    kv = [tiles(ukv[:, :, n].reshape(lora, H * P)).reshape(H // 2, 2, P, lora) for n in range(2)]
    A["w_ukv"] = np.concatenate(kv, 1).transpose(0, 2, 1, 3).reshape(H // 2, P, 4 * lora)
    A["w_mo"] = tiles(f(mla_w_out)[0])
    fi = f(ffn_w_in)
    A["w_fi"] = np.concatenate([tiles(fi[l]).reshape(2, FT, P, D).transpose(1, 0, 2, 3).reshape(2 * FT, P, D)
                                for l in range(2)], 0)
    fo = f(ffn_w_out)
    A["w_fo"] = np.concatenate([tiles(fo[l, h * HF * P:(h + 1) * HF * P]) for l in range(2) for h in range(2)], 0)
    A["w_fo"] = A["w_fo"].reshape(4 * KT, P, HF * P)
    taps = np.concatenate([f(ffn_conv_w), f(ffn_conv_b)[:, None]], 1)
    A["conv_w"] = taps.reshape(2, 4, 2, FT, P).transpose(4, 0, 3, 2, 1).reshape(P, 2, 2 * FT, 4)
    A["conv_old"] = f(state_conv)[:, 0].reshape(2, 2, 2, FT, P).transpose(4, 0, 3, 2, 1).reshape(P, 2, 2 * FT, 2)
    A["lat_w"] = np.stack([f(mla_q_norm_w)[0], f(mla_kv_norm_w)[0]]).reshape(2, LATENT, P).transpose(2, 0, 1)
    A["cache"] = rows(f(cache_ckv)[0, 0].T)
    A["cache_kpe"] = f(cache_kpe)[0, 0].T
    A["ident"] = np.eye(P, dtype=np.float32)
    p = np.arange(P)
    A["swap"] = (p[:, None] == (p ^ 32)[None]).astype(np.float32)
    pos = np.concatenate([np.arange(TP), PAST + np.arange(TS)]).astype(np.float32)
    inv = (np.float32(10000.0) ** (-np.arange(32, dtype=np.float32) / np.float32(32))).astype(np.float32)
    ang = (pos[None] * inv[p % 32][:, None]).astype(np.float32)
    A["cos"] = np.cos(ang).astype(np.float32)
    A["sin"] = (np.sin(ang) * np.where(p % 64 < 32, -1, 1)[:, None]).astype(np.float32)
    q = np.arange(P)[:, None]
    A["chunk_mask"] = np.concatenate([np.where(np.arange(P)[None] // 64 > q // 64, NEGATIVE, 0),
                                      np.where(np.arange(TP)[None] // 64 > (q + P) // 64, NEGATIVE, 0)], 1).astype(np.float32)
    lm = np.zeros((P, LEVELS, 64), np.float32)
    for l in range(LEVELS):
        half = 2 ** l
        b = np.arange(64) // half
        lm[:, l] = (p[:, None] // half == 2 * b[None])
    A["level_mask"] = lm
    carry = np.ones((P, T), np.float32)
    carry[:, [0, P, TP]] = 0
    A["carry"] = carry

    outs = {"o_y": (P, KT, T), "o_hp": (H, P, P), "o_hs": (H, P, P), "o_ckv": (P, LATENT, T), "o_kpe": (64, T),
            "o_conv": (2, P, 2 * FT, 4)}
    nc = _bacc.Bacc("TRN2", target_bir_lowering=False, num_devices=1)
    arrays, args = {}, {}
    for name, v in A.items():
        v = np.ascontiguousarray(v)
        arrays["in_" + name] = v
        args[name] = nc.dram_tensor("in_" + name, v.shape, mybir.dt.from_np(v.dtype), kind="ExternalInput").ap()
    for name, shape in outs.items():
        args[name] = nc.dram_tensor(name, shape, F32, kind="ExternalOutput").ap()
    trunk_program(nc, args)
    got = _run(nc, [arrays], core_ids=[0]).results[0]

    y = got["o_y"].transpose(2, 1, 0).reshape(T, D)
    ckv = got["o_ckv"].transpose(2, 1, 0).reshape(T, lora)
    kpe = got["o_kpe"].T
    conv = got["o_conv"].reshape(2, P, FT, 2, 2, 2).transpose(0, 4, 5, 3, 2, 1).reshape(2, 2, 2, 2 * FF)
    return (y[None, :TP], y[None, TP:], got["o_hp"][None, None], got["o_hs"][None, None],
            ckv[None, None, :TP], ckv[None, None, TP:], kpe[None, None, :TP], kpe[None, None, TP:],
            conv[:, 0][:, None], conv[:, 1][:, None])
```

```python
import math
from contextlib import ExitStack

import concourse.bass as bass
from concourse import mybir

F32 = mybir.dt.float32
F32R = mybir.dt.float32r
ALU = mybir.AluOpType
ACT = mybir.ActivationFunctionType
AX_X = mybir.AxisListType.X

P = 128
TP = 256
TS = 32
T = TP + TS
PAST = 128
TK = TP + PAST + TS
EPS = 1e-6
LEVELS = 7
RING = 4
UNITS = 8
LATENT = 4
EXP_LN_SET = 6
SILU_SET = 18
EXP_MAX = 2.0 ** 63
NEGATIVE = -1e30


def pieces(kt):
    return [(a, min(UNITS, kt - a)) for a in range(0, kt, UNITS)]


def trunk_program(nc, a):
    D = a["x"].shape[1] * P
    KT = D // P
    HEADS = KT
    FT = 2 * (a["w_fo"].shape[2] // P)
    HF = FT // 2
    PAIRS = HEADS // 2
    SCALE = float(P + 64) ** -0.5
    PK, PH = pieces(KT), pieces(HF)
    assert HF % 2 == 0 and KT % 4 == 0

    gemm4 = [(t, s, n) for t in range(4) for s, n in PK]
    out4 = [(t, s, n) for t in range(4) for s, n in PH]
    order = [("hgrn_in", HEADS, gemm4, 4), ("hgrn_out", KT // 4, gemm4, 4)]
    for layer in range(2):
        if layer == 1:
            order += [("down", 1, [(t, s, n) for t in range(9) for s, n in PK], 9),
                      ("pairs", PAIRS, [(0, 0, 8), (1, 8, 4), (2, 0, 8), (3, 8, 8)], 7),
                      ("mla_out", KT // 4, gemm4, 4)]
        for half in range(2):
            order += [(f"ffn_in{layer}{half}", HF // 2, gemm4, 4), (f"ffn_out{layer}{half}", KT // 4, out4, 4)]
    chunk0, tile0, c, t = {}, {}, 0, 0
    for name, trips, chunks, tiles in order:
        chunk0[name], tile0[name] = c, t
        c, t = c + trips * len(chunks), t + trips * tiles
    CHUNKS = {name: chunks for name, _, chunks, _ in order}
    assert len(PK) == 2
    first4 = [(t, s, n) for s, n in PK for t in range(4)]
    FIRST = {name: first4 + CHUNKS[name][8:] for name in
             ("hgrn_in", "hgrn_out", "down", "mla_out", "ffn_in00", "ffn_in10")}
    NEXT = {order[n][0]: order[n + 1][0] for n in range(len(order) - 1)}
    TILES = {name: tiles for name, _, _, tiles in order}

    def chunks_of(phase, i):
        return FIRST[phase] if phase in FIRST and isinstance(i, int) and i == 0 else CHUNKS[phase]

    class Chunk:
        def __init__(self, phase, i, k):
            n = len(CHUNKS[phase])
            at = chunk0[phase] + k
            self.first = isinstance(i, int) and at + i * n < RING
            self.slot = (at + (i * n if isinstance(i, int) else 0)) % RING
            assert isinstance(i, int) or n % RING == 0
            self.number = i * n + at
            if isinstance(i, int):
                self.load = (at + i * n) // RING
            else:
                self.load = i * (n // RING) + at // RING
            self.tile, self.start, self.units = chunks_of(phase, i)[k]

    def tile_number(phase, i, t):
        return i * TILES[phase] + (tile0[phase] + t)

    with ExitStack() as ctx:
        def sb(name, shape, dt=F32):
            return ctx.enter_context(nc.sbuf_tensor(name, shape, dt))

        def sem(name):
            return ctx.enter_context(nc.semaphore(name))

        psum = [ctx.enter_context(nc.psum_tensor(f"bank{n}", [P, 512], F32)) for n in range(8)]

        raw = sb("raw", [P, RING, UNITS * P])
        w_hi = sb("w_hi", [P, RING, UNITS * P], F32R)
        w_lo = sb("w_lo", [P, RING, UNITS * P], F32R)
        X = sb("X", [P, KT, T])
        h_hi = sb("h_hi", [P, max(KT * T, LATENT * (T + TK))], F32R)
        h_lo = sb("h_lo", [P, max(KT * T, LATENT * (T + TK))], F32R)
        taken = {"mixer": 0, "ffn": 0}
        with ExitStack() as mixer:
            def sbm(name, shape, dt=F32):
                taken["mixer"] += 4 * math.prod(shape[1:])
                return mixer.enter_context(nc.sbuf_tensor(name, shape, dt))
            o_hi = sbm("o_hi", [P, KT, T], F32R)
            o_lo = sbm("o_lo", [P, KT, T], F32R)
            row_tiles = sbm("row_tiles", [P, 10, T])
            qraw, graw, vfm, key, query, gate, fgate, qb, ke, diag = (row_tiles[:, n, :] for n in range(10))
            vtok, ktok = sbm("vtok", [P, 3, P]), sbm("ktok", [P, 3, P])
            lev = sbm("lev", [P, 2, LEVELS * 64])
            lev_s = sbm("lev_s", [TS, 5, 16])
            s_old, s_mid = sbm("s_old", [P, P]), sbm("s_mid", [P, P])
            s_new = sbm("s_new", [P, 2, P])
        EXT = T + 4
        with ExitStack() as ffn:
            def sbf(name, shape, dt=F32):
                taken["ffn"] += 4 * math.prod(shape[1:])
                return ffn.enter_context(nc.sbuf_tensor(name, shape, dt))
            g_hi = sbf("g_hi", [P, HF, T], F32R)
            g_lo = sbf("g_lo", [P, HF, T], F32R)
            ext = sbf("ext", [P, 4, EXT])
            cv = sbf("cv", [P, 4, T + 2])
            prod = sbf("prod", [P, 2, T])
        sb("shared", [P, max(taken.values()) // 4])
        Y = sb("Y", [P, max(KT, 16), T])
        yt = sb("yt", [P, 4, T])
        ssq = sb("ssq", [P, T])
        ssx = sb("ssx", [P, T])
        ones = sb("ones", [P, P])
        ident = sb("ident", [P, P])
        swap = sb("swap", [P, P])
        cos = sb("cos", [P, T])
        sin = sb("sin", [P, T])
        chunk_mask = sb("chunk_mask", [P, 3 * P])
        level_mask_f = sb("level_mask", [P, LEVELS, 64])
        level_mask = level_mask_f[:].rearrange("p l t -> p (l t)")
        carry = sb("carry", [P, T])
        eps = sb("eps", [P, 1])
        norm_w = sb("norm_w", [P, 2, 4, KT])
        lat_w = sb("lat_w", [P, 2, LATENT])
        gnorm_w = sb("gnorm_w", [P, 1])
        lbl = sb("lbl", [P, 3, HEADS])
        lbt = sb("lbt", [P, 4, HEADS])
        lb = sb("lb", [P, HEADS])
        oml = sb("oml", [P, HEADS])
        conv_w = sb("conv_w", [P, 2, 2 * FT, 4])
        conv_old = sb("conv_old", [P, 2, 2 * FT, 2])
        conv_new = sb("conv_new", [P, 2 * FT, 4])
        small = sb("small", [P, 3, T])

        LR, RSA, RSB = small[:, 0, :], small[:, 1, :], small[:, 2, :]
        H_HI = h_hi[:, 0:KT * T].rearrange("p (k t) -> p k t", t=T)
        H_LO = h_lo[:, 0:KT * T].rearrange("p (k t) -> p k t", t=T)

        loaded = [sem(f"loaded{n}") for n in range(RING)]
        consts_in, norm_w_in = sem("consts_in"), sem("norm_w_in")
        x_in = [sem(f"x_in{n}") for n in range(4)]
        hi_done, lo_done, chunk_done = sem("hi_done"), sem("lo_done"), sem("chunk_done")
        evacuated = sem("evacuated")
        filled = sem("filled")
        n_sum, n_log, n_rstd = sem("n_sum"), sem("n_log"), sem("n_rstd")
        y_scaled, x_ready = sem("y_scaled"), sem("x_ready")
        x_squared, x_added = sem("x_squared"), sem("x_added")
        n_hi, h_ready = sem("n_hi"), sem("h_ready")
        STAT = 5
        IN = "hgrn_in"
        block = None

        def ring_load(sp, w, phase, i, k, index):
            ch = Chunk(phase, i, k)
            if not ch.first:
                sp.wait_ge(lo_done, ch.number - (RING - 1))
            src = w[bass.ds(index, 1), :, ch.start * P:(ch.start + ch.units) * P].rearrange("a p n -> p (a n)")
            sp.dma_start(raw[:, ch.slot, 0:ch.units * P], src).then_inc(loaded[ch.slot], 16)

        def split_hi(act, phase, i, k):
            ch = Chunk(phase, i, k)
            act.wait_ge(loaded[ch.slot], 16 * (ch.load + 1))
            if not ch.first:
                act.wait_ge(chunk_done, ch.number - (RING - 1))
            n = ch.units * P
            act.activation(w_hi[:, ch.slot, 0:n], raw[:, ch.slot, 0:n], ACT.Copy).then_inc(hi_done, 1)

        def split_lo(dve, phase, i, k):
            ch = Chunk(phase, i, k)
            dve.wait_ge(hi_done, ch.number + 1)
            n = ch.units * P
            dve.tensor_tensor(w_lo[:, ch.slot, 0:n], raw[:, ch.slot, 0:n], w_hi[:, ch.slot, 0:n].bitcast(F32),
                              ALU.subtract).then_inc(lo_done, 1)

        def product(pe, out, ch, unit, rhs_hi, rhs_lo, start, stop):
            w = slice(unit * P, (unit + 1) * P)
            pe.matmul(out, w_hi[:, ch.slot, w], rhs_hi, start=start, stop=False)
            pe.matmul(out, w_hi[:, ch.slot, w], rhs_lo, start=False, stop=False)
            return pe.matmul(out, w_lo[:, ch.slot, w], rhs_hi, start=False, stop=stop)

        def tile_chunks(phase, i, t):
            return [k for k, (tt, _, _) in enumerate(chunks_of(phase, i)) if tt == t]

        def to_split(phase, i, t):
            if isinstance(i, int) and i == 0:
                if phase in FIRST and t < 4:
                    return [4, 5, 6, 7] if t == 0 and phase not in ("hgrn_out", "mla_out") else []
                return [k for k in tile_chunks(phase, i, t) if k >= 4]
            return tile_chunks(phase, i, t)

        def split_next(eng, split, phase, ks):
            if phase in NEXT:
                for k in ks:
                    split(eng, NEXT[phase], 0, k)

        def gemm_chunk(pe, phase, i, k, hi, lo, kt, ready=None):
            ch = Chunk(phase, i, k)
            if ch.start == 0 and not (isinstance(i, int) and i * TILES[phase] + ch.tile < 4):
                pe.wait_ge(evacuated, tile_number(phase, i, ch.tile) - 3)
            pe.wait_ge(lo_done, ch.number + 1)
            bank = psum[(ch.tile + (i * TILES[phase] if isinstance(i, int) else 0)) % 4]
            for u in range(ch.units):
                kk = ch.start + u
                if ready is not None:
                    pe.wait_ge(ready[0], ready[1] + (kk + 1))
                mm = product(pe, bank[:, 0:T], ch, u, hi[:, kk, :], lo[:, kk, :], kk == 0, kk == kt - 1)
            mm.then_inc(chunk_done, 1)

        def last_chunk(phase, i, t):
            return Chunk(phase, i, tile_chunks(phase, i, t)[-1]).number + 1

        def gemm_first(pe, phase, s):
            a0, a1 = Chunk(phase, 0, 0), Chunk(phase, 0, 1)
            for ch in (a0, a1):
                if phase != IN:
                    pe.wait_ge(evacuated, tile_number(phase, 0, ch.tile) - 3)
                pe.wait_ge(lo_done, ch.number + 1)
            for kk in range(a0.units):
                pe.wait_ge(h_ready, KT * s + kk + 1)
                for ch in (a0, a1):
                    mm = product(pe, psum[ch.tile][:, 0:T], ch, kk, H_HI[:, kk, :], H_LO[:, kk, :], kk == 0, False)
                    if kk == a0.units - 1:
                        mm.then_inc(chunk_done, 1)
            for k in range(2, 8):
                gemm_chunk(pe, phase, 0, k, H_HI, H_LO, KT, (h_ready, KT * s) if k == 4 else None)
                if k == 5:
                    pe.wait_ge(x_added, KT * (s + 1))
                    pe.matmul(psum[STAT][:, 0:T], ones[:], ssx[:], start=True, stop=True).then_inc(n_sum, 1)

        def gemm_late(pe, phase, part, hi, lo, done, counts):
            if part == 0:
                pe.wait_ge(evacuated, tile_number(phase, 0, 0))
            if part < 4:
                gemm_chunk(pe, phase, 0, part, hi, lo, KT)
            elif part < 8:
                ch = Chunk(phase, 0, part)
                pe.wait_ge(lo_done, ch.number + 1)
                if part == 4:
                    pe.wait_ge(done, counts[0])
                for kk in range(ch.start, KT - 2):
                    product(pe, psum[ch.tile][:, 0:T], ch, kk - ch.start, hi[:, kk, :], lo[:, kk, :], False, False)
            else:
                kk = KT - 2 + (part - 8)
                pe.wait_ge(done, counts[part - 7])
                for k in range(4, 8):
                    ch = Chunk(phase, 0, k)
                    mm = product(pe, psum[ch.tile][:, 0:T], ch, kk - ch.start, hi[:, kk, :], lo[:, kk, :], False, kk == KT - 1)
                    if kk == KT - 1:
                        mm.then_inc(chunk_done, 1)

        hg = ctx.enter_context(ExitStack())

        class HG:
            base = Y[:, :, :].rearrange("p k t -> p (k t)")
            Z = base[:, 0:LEVELS * T]
            o = LEVELS * T
            EX = base[:, o:o + 3 * T]
            SG = base[:, o + 3 * T:o + 6 * T]
            B = base[:, o + 6 * T:o + 7 * T]
            EB = base[:, o + 7 * T:o + 8 * T]
            EE = base[:, o + 8 * T:o + 9 * T]
        assert 16 * T >= (LEVELS + 9) * T
        on = yt[:, 0, :]
        o_sq = yt[:, 1, :]
        t1 = yt[:, 2, :]

        names = ["scaled", "exps", "clamped", "logs", "sigmoids", "fgates", "keys", "gates", "logf", "decays", "ends_exp", "diffs",
                 "diffs_exp", "ke_ready", "pairs_ready", "v_turned", "v_tok", "k_turned", "k_tok", "levels_done",
                 "att_ready", "updates", "mid_state", "states", "o_raw", "o_squared", "o_summed", "o_logs", "o_rstd", "o_scaled",
                 "o_ready", "o_hi", "o_done", "s_loaded", "s_stored", "lb_ready"]
        S = {n: sem("h_" + n) for n in names}
        TR, LVA, LVB, DG = psum[4], psum[5], psum[6], psum[7]
        OV, SU, GS = psum[7], psum[5], psum[6]
        BLOCKS = [(0, P), (P, P), (TP, TS)]

        def halves(ap, m):
            v = ap.rearrange("p (b two m) -> p b two m", two=2, m=m)
            return v[:, :, 0, :], v[:, :, 1, :]

        def ref_col(m, n):
            v = HG.B[:, 0:n].rearrange("p (b two m) -> p b two m", two=2, m=m)
            return v[:, :, 0, m - 1:m].to_broadcast([P, n // (2 * m), m])

        def level_span(l):
            return T if 2 ** l < TS else TP

        def on_position(split, eng, j, k):
            if isinstance(j, int) and j == HEADS:
                split(eng, "hgrn_out", 0, k)
            elif not (isinstance(j, int) and j > HEADS):
                split(eng, IN, j, k)

        def hgrn_act(act, j, gemm, main, tail):
            r, t = j - 1, j - 2
            hi = lambda k: on_position(split_hi, act, j, k)
            hi(0); hi(1)
            if main:
                act.wait_ge(chunk_done, last_chunk(IN, r, 2))
                if not isinstance(r, int) or r > 0:
                    act.wait_ge(S["v_turned"], r)
                act.activation(vfm[:], psum[2][:, 0:T], ACT.Copy).then_inc(evacuated, 1)
            hi(2); hi(3)
            if main:
                act.wait_ge(chunk_done, last_chunk(IN, r, 3))
                act.activation(graw[:], psum[3][:, 0:T], ACT.Copy).then_inc(evacuated, 1)
            if tail:
                act.wait_ge(S["k_turned"], t + 1)
                act.activation(ktok[:, 0:2, :], TR[:, 0:2 * P], ACT.Copy)
                act.activation(ktok[0:TS, 2, :], TR[0:TS, 2 * P:3 * P], ACT.Copy).then_inc(S["k_tok"], 1)
            hi(4)
            if main:
                act.wait_ge(S["scaled"], 4 * r + 4)
                act.activation(HG.EX[:, 0:T], HG.EX[:, 0:T], ACT.Exp, scale=-1.0)
                act.activation(HG.EX[:, T:2 * T], qraw[:], ACT.Exp, scale=-1.0)
                act.activation(HG.EX[:, 2 * T:3 * T], graw[:], ACT.Exp, scale=-1.0).then_inc(S["exps"], 1)
                act.wait_ge(S["clamped"], r + 1)
                act.activation(HG.SG, HG.EX, ACT.Ln, bias=1.0).then_inc(S["logs"], 1)
                act.wait_ge(S["logs"], r + 1)
                act.activation(HG.SG, HG.SG, ACT.Exp, scale=-1.0).then_inc(S["sigmoids"], 1)
            hi(5)
            if main:
                act.wait_ge(S["fgates"], r + 1)
                act.activation(fgate[:], fgate[:], ACT.Ln).then_inc(S["logf"], 1)
            hi(6)
            if tail:
                act.wait_ge(S["o_raw"], t + 1)
                act.activation(o_sq, OV[:, 0:T], ACT.Square).then_inc(S["o_squared"], 1)
                act.wait_ge(S["states"], t + 1)
                for n, out in enumerate((a["o_hp"], a["o_hs"])):
                    act.dma_start(out[bass.ds(t, 1), :, :].rearrange("h k v -> k (h v)"), s_new[:, n, :])\
                        .then_inc(S["s_stored"], 16)
                if not isinstance(t, int) or t < HEADS - 1:
                    state_load(act, t + 1)
            if main:
                act.wait_ge(S["v_turned"], r + 1)
                act.activation(vtok[:, 0:2, :], TR[:, 0:2 * P], ACT.Copy)
                act.activation(vtok[0:TS, 2, :], TR[0:TS, 2 * P:3 * P], ACT.Copy).then_inc(S["v_tok"], 1)
                act.wait_ge(S["decays"], r + 1)
                if not isinstance(r, int) or r > 0:
                    act.wait_ge(S["states"], r)
                act.activation(HG.EB, HG.B, ACT.Exp)
                for n, (b0, bn) in enumerate(BLOCKS):
                    e = act.activation(HG.EE[:, b0:b0 + bn], HG.B[:, b0:b0 + bn], ACT.Exp, scale=-1.0,
                                       bias=HG.B[:, b0 + bn - 1:b0 + bn])
                e.then_inc(S["ends_exp"], 1)
            hi(7)
            if main:
                act.wait_ge(S["diffs"], r + 1)
                act.activation(HG.Z[:, 0:5 * T], HG.Z[:, 0:5 * T], ACT.Exp)
                v = HG.Z[:, 5 * T:7 * T].rearrange("p (l t) -> p l t", l=2)[:, :, 0:TP]
                act.activation(v, v, ACT.Exp).then_inc(S["diffs_exp"], 1)
            if tail:
                act.wait_ge(S["o_summed"], t + 1)
                act.activation(LR, GS[:, 0:T], ACT.Ln, scale=1.0 / P, bias=eps[:, 0:1]).then_inc(S["o_logs"], 1)
                act.wait_ge(S["o_logs"], t + 1)
                act.activation(RSA, LR, ACT.Exp, scale=-0.5).then_inc(S["o_rstd"], 1)
            if gemm:
                act.wait_ge(chunk_done, last_chunk(IN, j, 0))
                if main:
                    act.wait_ge(S["gates"], r + 1)
                act.activation(HG.EX[:, 0:T], psum[0][:, 0:T], ACT.Copy).then_inc(evacuated, 1)
                act.wait_ge(chunk_done, last_chunk(IN, j, 1))
                act.activation(qraw[:], psum[1][:, 0:T], ACT.Copy).then_inc(evacuated, 1)
            if tail:
                act.wait_ge(S["o_ready"], t + 1)
                act.activation(o_hi[:, bass.ds(t, 1), :], on.unsqueeze(1), ACT.Copy).then_inc(S["o_hi"], 1)

        def hgrn_dve(dve, j, gemm, main, tail):
            r, t = j - 1, j - 2
            lo = lambda k: on_position(split_lo, dve, j, k)
            lo(0); lo(1); lo(2); lo(3)
            if tail:
                dve.wait_ge(S["levels_done"], t + 1)
                for n, lv in enumerate((LVA, LVB)):
                    dve.tensor_tensor(lev[:, n, :], lv[:, 0:LEVELS * 64], level_mask, ALU.mult)
                dve.tensor_tensor(diag[:, 0:TP].rearrange("p (n t) -> p n t", n=2), DG[:, 0:TP].rearrange("p (n t) -> p n t", n=2),
                                  ident[:].unsqueeze(1).to_broadcast([P, 2, P]), ALU.mult)
                dve.tensor_tensor(diag[0:TS, TP:T], DG[0:TS, TP:T], ident[0:TS, 0:TS], ALU.mult)
                dve.tensor_tensor(lev_s[:], DG[0:TS, T:T + 5 * 16].rearrange("p (l t) -> p l t", l=5),
                                  level_mask_f[0:TS, 0:5, 0:16], ALU.mult).then_inc(S["att_ready"], 1)
            lo(4)
            if main:
                dve.wait_ge(S["exps"], r + 1)
                dve.tensor_scalar(HG.EX, HG.EX, EXP_MAX, None, ALU.min).then_inc(S["clamped"], 1)
                dve.wait_ge(S["sigmoids"], r + 1)
                dve.tensor_scalar(fgate[:], HG.SG[:, 0:T], oml[:, bass.ds(r, 1)], lb[:, bass.ds(r, 1)],
                                  ALU.mult, ALU.add).then_inc(S["fgates"], 1)
                if not isinstance(r, int) or r > 0:
                    dve.wait_ge(S["levels_done"], r)
                dve.scalar_tensor_tensor(out=key[:], in0=HG.SG[:, 0:T], scalar=oml[:, bass.ds(r, 1)],
                                         in1=HG.EX[:, 0:T], op0=ALU.mult, op1=ALU.mult)
                dve.tensor_tensor(query[:], qraw[:], HG.SG[:, T:2 * T], ALU.mult)
            lo(5)
            if tail:
                dve.wait_ge(S["updates"], t + 1)
                if not isinstance(t, int) or t > 0:
                    dve.wait_ge(S["s_stored"], 32 * t)
                    dve.wait_ge(S["o_raw"], t)
                dve.wait_ge(S["s_loaded"], 16 * (t + 1))
                dve.tensor_copy(s_mid[:], SU[:, 0:P]).then_inc(S["mid_state"], 1)
                dve.scalar_tensor_tensor(out=s_new[:, 1, :], in0=s_old[:], scalar=HG.EB[:, T - 1:T],
                                         in1=SU[:, 2 * P:3 * P], op0=ALU.mult, op1=ALU.add)
                dve.wait_ge(S["mid_state"], t + 1)
                dve.scalar_tensor_tensor(out=s_new[:, 0, :], in0=s_mid[:], scalar=HG.EB[:, TP - 1:TP],
                                         in1=SU[:, P:2 * P], op0=ALU.mult, op1=ALU.add).then_inc(S["states"], 1)
            if main:
                dve.wait_ge(S["logf"], r + 1)
                dve.tensor_tensor_scan(HG.B, carry[:], fgate[:], 0.0, ALU.mult, ALU.add).then_inc(S["decays"], 1)
            lo(6)
            if main:
                dve.wait_ge(S["decays"], r + 1)
                for l in range(LEVELS):
                    m, n = 2 ** l, level_span(l)
                    zf, zs = halves(HG.Z[:, l * T:l * T + n], m)
                    bf, bs = halves(HG.B[:, 0:n], m)
                    dve.tensor_tensor(zf, ref_col(m, n), bf, ALU.subtract)
                    z = dve.tensor_tensor(zs, bs, ref_col(m, n), ALU.subtract)
                z.then_inc(S["diffs"], 1)
            lo(7)
            if main:
                dve.wait_ge(S["ends_exp"], r + 1)
                dve.tensor_tensor(qb[:], query[:], HG.EB, ALU.mult)
                dve.tensor_tensor(ke[:], key[:], HG.EE, ALU.mult).then_inc(S["ke_ready"], 1)
            if tail:
                dve.wait_ge(S["o_rstd"], t + 1)
                dve.scalar_tensor_tensor(out=t1, in0=gate[:], scalar=gnorm_w[:, 0:1], in1=RSA,
                                         op0=ALU.mult, op1=ALU.mult).then_inc(S["o_scaled"], 1)
                dve.wait_ge(S["o_scaled"], t + 1)
                dve.tensor_tensor(on, t1, OV[:, 0:T], ALU.mult).then_inc(S["o_ready"], 1)
            if main:
                dve.tensor_tensor(gate[:], graw[:], HG.SG[:, 2 * T:3 * T], ALU.mult).then_inc(S["gates"], 1)
                dve.wait_ge(S["diffs_exp"], r + 1)
                for l in range(LEVELS):
                    m, n = 2 ** l, level_span(l)
                    zf, zs = halves(HG.Z[:, l * T:l * T + n], m)
                    dve.tensor_tensor(zf, zf, halves(key[:, 0:n], m)[0], ALU.mult)
                    z = dve.tensor_tensor(zs, zs, halves(query[:, 0:n], m)[1], ALU.mult)
                z.then_inc(S["pairs_ready"], 1)
            if tail:
                dve.wait_ge(S["o_hi"], t + 1)
                dve.tensor_tensor(o_lo[:, bass.ds(t, 1), :], on.unsqueeze(1), o_hi[:, bass.ds(t, 1), :].bitcast(F32),
                                  ALU.subtract).then_inc(S["o_done"], 1)

        def hgrn_pe(pe, j, gemm, main, tail):
            r, t = j - 1, j - 2

            def mm(k):
                if gemm:
                    gemm_chunk(pe, IN, j, k, H_HI, H_LO, KT)
                elif isinstance(j, int) and j == HEADS:
                    late(k)

            def late(k):
                gemm_late(pe, "hgrn_out", k, o_hi, o_lo, S["o_done"], (HEADS - 2, HEADS - 1, HEADS))
            mm(0); mm(1)
            if main:
                pe.wait_ge(S["scaled"], 4 * r + 3)
                if tail:
                    pe.wait_ge(S["k_tok"], t + 1)
                for n, (b0, bn) in enumerate(BLOCKS):
                    tr = pe.transpose(TR[0:bn, n * P:(n + 1) * P], vfm[:, b0:b0 + bn], ident[:])
                tr.then_inc(S["v_turned"], 1)
            if tail:
                pe.wait_ge(S["k_tok"], t + 1)
                pe.wait_ge(S["att_ready"], t + 1)
            mm(2)
            if tail:
                for n, (b0, bn) in enumerate(BLOCKS):
                    su = pe.matmul(SU[:, n * P:(n + 1) * P], ktok[0:bn, n, :], vtok[0:bn, n, :], start=True, stop=True)
                su.then_inc(S["updates"], 1)
            mm(3)
            if isinstance(j, int) and j == HEADS + 1:
                late(8)
            if tail:
                pe.wait_ge(S["states"], t + 1)
                for n, (b0, bn) in enumerate(BLOCKS):
                    v = vtok[0:bn, n, :]
                    for l in range(LEVELS if n < 2 else 5):
                        scores = lev[:, n, l * 64:l * 64 + 64] if n < 2 else lev_s[:, l, :]
                        pe.matmul(halves(OV[:, b0:b0 + bn], 2 ** l)[1], v, scores, start=(l == 0), stop=False,
                                  skip_group_check=True)
                    if n > 0:
                        pe.matmul(OV[:, b0:b0 + bn], (s_mid, s_old)[n - 1][:], qb[:, b0:b0 + bn], start=False, stop=False,
                                  skip_group_check=True)
                    ov = pe.matmul(OV[:, b0:b0 + bn], v, diag[0:bn, b0:b0 + bn], start=False, stop=True,
                                   skip_group_check=True)
                ov.then_inc(S["o_raw"], 1)
            mm(4)
            mm(5)
            if tail:
                pe.wait_ge(S["o_squared"], t + 1)
                pe.matmul(GS[:, 0:T], ones[:], o_sq, start=True, stop=True).then_inc(S["o_summed"], 1)
            mm(6)
            if main:
                pe.wait_ge(S["ke_ready"], r + 1)
                pe.wait_ge(S["v_tok"], r + 1)
                for n, (b0, bn) in enumerate(BLOCKS):
                    tr = pe.transpose(TR[0:bn, n * P:(n + 1) * P], ke[:, b0:b0 + bn], ident[:])
                tr.then_inc(S["k_turned"], 1)
            mm(7)
            if main:
                pe.wait_ge(S["pairs_ready"], r + 1)
                if tail:
                    pe.wait_ge(S["o_ready"], t + 1)
                for b0, lv in ((0, LVA), (P, LVB)):
                    for l in range(LEVELS):
                        z = HG.Z[:, l * T + b0:l * T + b0 + P]
                        pe.matmul(lv[:, l * 64:l * 64 + 64], z, halves(z, 2 ** l)[1], start=True, stop=True)
                    pe.matmul(DG[:, b0:b0 + P], key[:, b0:b0 + P], query[:, b0:b0 + P], start=True, stop=True)
                for l in range(5):
                    z = HG.Z[:, l * T + TP:l * T + T]
                    pe.matmul(DG[0:TS, T + l * 16:T + l * 16 + 16], z, halves(z, 2 ** l)[1], start=True, stop=True)
                pe.matmul(DG[0:TS, TP:T], key[:, TP:T], query[:, TP:T], start=True, stop=True)\
                    .then_inc(S["levels_done"], 1)
            if isinstance(j, int) and j == HEADS + 1:
                late(9)

        def hgrn_pool(pool, j):
            for t, x in enumerate((HG.EX[:, 0:T], qraw, vfm, graw)):
                pool.wait_ge(evacuated, tile_number(IN, j, t) + 1)
                pool.tensor_tensor(x, x, RSB, ALU.mult).then_inc(S["scaled"], 1)

        def state_load(eng, t):
            eng.dma_start(s_old[:], a["s_in"][bass.ds(t, 1), :, :].rearrange("h k v -> k (h v)")).then_inc(S["s_loaded"], 16)

        def run_hgrn(eng, step, first):
            first(eng)
            step(eng, 1, True, True, False)
            step(eng, 2, True, True, True)
            with eng.Fori(3, HEADS) as j:
                step(eng, j, True, True, True)
            step(eng, HEADS, False, True, True)
            step(eng, HEADS + 1, False, False, True)

        y_kept, y_squared = sem("y_kept"), sem("y_squared")
        sq = sb("sq", [P, T])
        y_done = sem("y_done")
        y_count = {}
        sq_count = {}
        n_kept = n_sq = 0
        n_done = 4
        for name, trips, _, tiles in order:
            if "out" in name or "down" in name:
                mode = {"hgrn_out": "only", "mla_out": "only", "down": "first"}.get(name)
                mode = mode or ("first" if name.endswith("0") else "add")
                y_count[name] = (n_done, n_kept, n_sq, mode)
                n_done += trips * tiles
                n_kept += trips * tiles if mode == "add" else 0
                n_sq += trips * tiles if mode != "first" else 0
        TRIPS = {name: trips for name, trips, _, _ in order}

        def out_act(act, phase, i, t):
            act.wait_ge(chunk_done, last_chunk(phase, i, t))
            n = y_count[phase][0] + t
            if "ffn" in phase and isinstance(i, int) and i == 0 and t == 0:
                act.wait_ge(f_scaled, f_tile(int(phase[-2]), int(phase[-1]), NI, 0) + 4)
            act.wait_ge(y_done, i * TILES[phase] + (n - 3))
            act.activation(yt[:, t % 4, :], psum[t % 4][:, 0:T], ACT.Copy).then_inc(evacuated, 1)

        def out_dve(dve, phase, i, t, col):
            done0, kept0, sq0, mode = y_count[phase]
            n = TILES[phase]
            dve.wait_ge(evacuated, tile_number(phase, i, t) + 1)
            ycol = Y[:, bass.ds(col, 1), :]
            if phase == "down":
                dve.tensor_tensor(ycol, yt[:, t % 4:t % 4 + 1, :], RSB.unsqueeze(1), ALU.mult).then_inc(y_done, 1)
                return
            if mode == "first":
                dve.tensor_copy(ycol, yt[:, t % 4:t % 4 + 1, :]).then_inc(y_done, 1)
                return
            dve.wait_ge(y_done, i * n + (done0 + t))
            if mode == "add":
                dve.tensor_tensor(ycol, ycol, yt[:, t % 4:t % 4 + 1, :], ALU.add).then_inc(y_kept, 1)
                dve.wait_ge(y_kept, i * n + (kept0 + t + 1))
                dve.tensor_tensor(sq[:].unsqueeze(1), ycol, ycol, ALU.mult).then_inc(y_squared, 1)
            else:
                dve.tensor_copy(ycol, yt[:, t % 4:t % 4 + 1, :])
                dve.tensor_tensor(sq[:], yt[:, t % 4, :], yt[:, t % 4, :], ALU.mult).then_inc(y_squared, 1)
            dve.wait_ge(y_squared, i * n + (sq0 + t + 1))
            dve.tensor_tensor(ssq[:], ssq[:], sq[:], ALU.add).then_inc(y_done, 1)

        def run_out(eng, phase, split, drain, stat=None):
            trips, n = TRIPS[phase], TILES[phase]

            def trip(i, before):
                for t in range(n):
                    for k in to_split(phase, i, t):
                        split(eng, phase, i, k)
                    if stat and isinstance(i, int) and i == 0 and t == 0:
                        stat(eng)
                    if t > 0 or before:
                        drain(eng, phase, i if t else i - 1, t - 1 if t else n - 1)
            trip(0, False)
            if trips > 2:
                with eng.Fori(1, trips) as i:
                    trip(i, True)
            elif trips == 2:
                trip(1, True)
            split_next(eng, split, phase, (0, 1, 2))
            drain(eng, phase, trips - 1, n - 1)
            split_next(eng, split, phase, (3,))

        def out_col(phase, i, t):
            return i * TILES[phase] + t

        def run_out_act(act, phase, stat=None):
            run_out(act, phase, split_hi, out_act, stat)

        def run_out_dve(dve, phase):
            if y_count[phase][3] != "first":
                dve.memset(ssq[:], 0.0).then_inc(filled_ssq, 1)
                dve.wait_ge(filled_ssq, 1 + [p for p in y_count if y_count[p][3] != "first"].index(phase))
            run_out(dve, phase, split_lo, lambda e, ph, i, t: out_dve(e, ph, i, t, out_col(ph, i, t)),
                    (lambda e: e.wait_ge(n_rstd, stat[2, "pre"] + 1)) if phase == "down" else None)

        filled_ssq = sem("filled_ssq")

        def run_out_pe(pe, phase, hi, lo, kt, first=0, ready=None):
            for k in range(first, len(CHUNKS[phase])):
                at_first = ready if ready and Chunk(phase, 0, k).tile == 0 else None
                gemm_chunk(pe, phase, 0, k, hi, lo, kt, at_first)
            if TRIPS[phase] > 1:
                with pe.Fori(1, TRIPS[phase]) as i:
                    for k in range(len(CHUNKS[phase])):
                        gemm_chunk(pe, phase, i, k, hi, lo, kt)

        stages = [(None, (0, 0)), ((0, 1), (0, 2)), ((0, 3), (1, 0)), ((1, 1), (1, 2)), ((1, 3), None)]
        stat = {}
        n = 0
        for s, (post, pre) in enumerate(stages):
            stat[s, "post"] = n
            n += post is not None
            stat[s, "pre"] = n
            n += pre is not None
        SQ = [sq[:], LR]

        def rstd(act, n, bank, out, width):
            act.wait_ge(n_sum, n + 1)
            act.activation(out, bank[:, 0:T], ACT.Ln, scale=1.0 / width, bias=eps[:, 0:1]).then_inc(n_log, 1)
            act.wait_ge(n_log, n + 1)
            act.activation(out, out, ACT.Exp, scale=-0.5).then_inc(n_rstd, 1)

        def load_set(act, number):
            act.add_instruction(mybir.InstLoadActFuncSet(act_func_set_id=number, name=nc.get_next_instruction_name(),
                                                         engine=mybir.EngineType.Activation))

        def pre_stat_act(act, s):
            rstd(act, stat[s, "pre"], psum[STAT], RSB, D)

        def norm_act(act, s):
            post, pre = stages[s]
            load_set(act, EXP_LN_SET)
            if post:
                rstd(act, stat[s, "post"], psum[4], RSA, D)
            if pre:
                lb_, wb = pre
                for k in range(KT):
                    q = KT * s + k
                    if s == 0:
                        act.wait_ge(x_in[k // 4], 16)
                    else:
                        act.wait_ge(x_ready, KT * (s - 1) + k + 1)
                    act.activation(H_HI[:, k, :], X[:, k, :], ACT.Copy, scale=norm_w[:, lb_, wb, k:k + 1]).then_inc(n_hi, 1)
                    if q >= 2:
                        act.wait_ge(x_added, q - 1)
                    act.activation(SQ[k % 2], X[:, k, :], ACT.Square).then_inc(x_squared, 1)

        def norm_pool(pool, s):
            for k in range(KT):
                q = KT * s + k
                pool.wait_ge(x_squared, q + 1)
                if k == 0:
                    pool.tensor_copy(ssx[:], SQ[0]).then_inc(x_added, 1)
                else:
                    pool.wait_ge(x_added, q)
                    pool.tensor_tensor(ssx[:], ssx[:], SQ[k % 2], ALU.add).then_inc(x_added, 1)

        def norm_pe(pe, s):
            last = [p for p in y_count][{1: 0, 2: 2, 3: 4, 4: 6}[s]]
            done0 = y_count[last][0] + TRIPS[last] * TILES[last]
            pe.wait_ge(y_done, done0)
            pe.matmul(psum[4][:, 0:T], ones[:], ssq[:], start=True, stop=True).then_inc(n_sum, 1)

        def norm_dve(dve, s):
            post, pre = stages[s]
            if post:
                la, wa = post
                dve.wait_ge(n_rstd, stat[s, "post"] + 1)
            for k in range(KT + 3):
                if post and k < KT:
                    dve.scalar_tensor_tensor(out=Y[:, k, :], in0=Y[:, k, :], scalar=norm_w[:, la, wa, k:k + 1], in1=RSA,
                                             op0=ALU.mult, op1=ALU.mult).then_inc(y_scaled, 1)
                if post and 1 <= k <= KT:
                    dve.wait_ge(y_scaled, KT * (s - 1) + k)
                    dve.tensor_tensor(X[:, k - 1, :], X[:, k - 1, :], Y[:, k - 1, :], ALU.add).then_inc(x_ready, 1)
                if pre and k >= 3:
                    lb_, wb = pre
                    c = k - 3
                    dve.wait_ge(n_hi, KT * s + c + 1)
                    dve.scalar_tensor_tensor(out=H_LO[:, c, :], in0=X[:, c, :], scalar=norm_w[:, lb_, wb, c:c + 1],
                                             in1=H_HI[:, c, :].bitcast(F32), op0=ALU.mult, op1=ALU.subtract)\
                        .then_inc(h_ready, 1)

        rows_done, conv_step, conv_done = sem("f_rows"), sem("f_conv_step"), sem("f_conv")
        f_scaled = sem("f_scaled")
        silu_done, prod_done, g_hi_done, g_done = sem("f_silu"), sem("f_prod"), sem("f_g_hi"), sem("f_g")
        conv_stored = sem("conv_stored")
        NI = HF // 2

        def ffn_base(layer, half):
            return 2 * layer + half

        def f_tile(layer, half, i, t):
            return i * 4 + (ffn_base(layer, half) * NI * 4 + t)

        def f_hid(layer, half, i, jj):
            return i * 2 + (ffn_base(layer, half) * NI * 2 + jj)

        def f_col(half, i, t):
            return i * 4 + (half * NI * 4 + t)

        def ffn_act(act, layer, half, i, gemm, prev):
            phase = f"ffn_in{layer}{half}"
            stats = half == 0 and isinstance(i, int) and i == 0
            before = {(0, 0): "hgrn_out", (0, 1): "ffn_out00", (1, 0): "mla_out", (1, 1): "ffn_out10"}[layer, half]
            y_before = y_count[before][0] + TRIPS[before] * TILES[before]

            def hi(t):
                if gemm:
                    for k in to_split(phase, i, t):
                        split_hi(act, phase, i, k)
                else:
                    split_next(act, split_hi, phase, ([0], [1], [2, 3])[t])

            def evac(i, t):
                act.wait_ge(chunk_done, last_chunk(phase, i, t))
                if isinstance(i, int) and i == 0:
                    act.wait_ge(y_done, y_before)
                else:
                    act.wait_ge(f_scaled, f_tile(layer, half, i, t) + 1)
                act.activation(yt[:, t, :], psum[t][:, 0:T], ACT.Copy).then_inc(evacuated, 1)

            def silu(i, jj):
                act.wait_ge(conv_done, f_tile(layer, half, i, 2 * jj) + 5)
                act.activation(cv[:, 2 * jj, :], cv[:, 2 * jj, :], ACT.Silu).then_inc(silu_done, 1)

            def g_top(i, jj):
                act.wait_ge(prod_done, f_hid(layer, half, i, jj) + 1)
                act.activation(g_hi[:, bass.ds(i * 2 + jj, 1), :], prod[:, jj:jj + 1, :], ACT.Copy).then_inc(g_hi_done, 1)

            hi(0)
            if stats:
                pre_stat_act(act, {0: 1, 2: 3}[ffn_base(layer, half)])
                load_set(act, SILU_SET)
            if prev:
                g_top(i - 1, 0)
                evac(i - 1, 2)
            hi(1)
            if prev:
                evac(i - 1, 3)
                silu(i - 1, 1)
            hi(2)
            if prev:
                g_top(i - 1, 1)
            if gemm:
                evac(i, 0)
                hi(3)
                evac(i, 1)
                silu(i, 0)

        def ffn_dve(dve, layer, half, i, gemm, prev):
            phase = f"ffn_in{layer}{half}"

            def lo(t):
                if gemm:
                    for k in to_split(phase, i, t):
                        split_lo(dve, phase, i, k)
                else:
                    split_next(dve, split_lo, phase, ([0], [1], [2, 3])[t])

            def conv(i, t):
                n = f_tile(layer, half, i, t)
                w = conv_w[:, layer, :, :].rearrange("p c w -> p (c w)")

                def tap(x):
                    return w[:, bass.ds(f_col(half, i, t) * 4 + x, 1)]
                dve.wait_ge(rows_done, n + 1)
                if not (isinstance(i, int) and i == 0 and ffn_base(layer, half) == 0):
                    dve.wait_ge(prod_done, f_hid(layer, half, i, t // 2))
                dve.tensor_scalar(cv[:, t, :], ext[:, t, 2:EXT], tap(2), tap(3), ALU.mult, ALU.add).then_inc(conv_step, 1)
                dve.wait_ge(conv_step, n * 2 + 1)
                dve.scalar_tensor_tensor(out=cv[:, t, :], in0=ext[:, t, 1:EXT - 1], scalar=tap(1), in1=cv[:, t, :],
                                         op0=ALU.mult, op1=ALU.add).then_inc(conv_step, 1)
                dve.wait_ge(conv_step, n * 2 + 2)
                dve.scalar_tensor_tensor(out=cv[:, t, :], in0=ext[:, t, 0:EXT - 2], scalar=tap(0), in1=cv[:, t, :],
                                         op0=ALU.mult, op1=ALU.add).then_inc(conv_done, 1)

            def gated(i, jj):
                dve.wait_ge(silu_done, f_hid(layer, half, i, jj) + 1)
                dve.wait_ge(conv_done, f_tile(layer, half, i, 2 * jj + 1) + 5)
                dve.tensor_tensor(prod[:, jj, 0:TP], cv[:, 2 * jj, 0:TP], cv[:, 2 * jj + 1, 0:TP], ALU.mult)
                dve.tensor_tensor(prod[:, jj, TP:T], cv[:, 2 * jj, TP + 2:T + 2], cv[:, 2 * jj + 1, TP + 2:T + 2],
                                  ALU.mult).then_inc(prod_done, 1)

            def g_rest(i, jj):
                dve.wait_ge(g_hi_done, f_hid(layer, half, i, jj) + 1)
                at = bass.ds(i * 2 + jj, 1)
                dve.tensor_tensor(g_lo[:, at, :], prod[:, jj:jj + 1, :], g_hi[:, at, :].bitcast(F32),
                                  ALU.subtract).then_inc(g_done, 1)

            lo(0)
            if prev:
                g_rest(i - 1, 0)
                conv(i - 1, 2)
            lo(1)
            if prev:
                conv(i - 1, 3)
                gated(i - 1, 1)
            lo(2)
            if gemm:
                conv(i, 0)
            if prev:
                g_rest(i - 1, 1)
            if gemm:
                lo(3)
                conv(i, 1)
                gated(i, 0)

        def ffn_pool(pool, layer, half, i):
            phase = f"ffn_in{layer}{half}"
            for t in range(4):
                pool.wait_ge(evacuated, tile_number(phase, i, t) + 1)
                pool.wait_ge(conv_done, f_tile(layer, half, i, t) + 1)
                pool.tensor_tensor(ext[:, t, 2:2 + TP], yt[:, t, 0:TP], RSB[:, 0:TP], ALU.mult)
                pool.tensor_tensor(ext[:, t, 4 + TP:EXT], yt[:, t, TP:T], RSB[:, TP:T], ALU.mult).then_inc(f_scaled, 1)
                at = bass.ds(f_col(half, i, t), 1)
                pool.tensor_copy(ext[:, t:t + 1, 2 + TP:4 + TP], conv_old[:, layer, at, :])
                pool.wait_ge(f_scaled, f_tile(layer, half, i, t) + 5)
                new = ext[:, t, EXT - 2 * (TS + 2):EXT].rearrange("p (s c) -> p s c", c=TS + 2)[:, :, TS:TS + 2]
                pool.tensor_copy(conv_new[:, at, :].rearrange("p a (s c) -> p (a s) c", c=2), new).then_inc(rows_done, 1)

        def run_ffn_in(eng, step, layer, half):
            step(eng, layer, half, 0, True, False)
            if half == 0:
                step(eng, layer, half, 1, True, True)
            with eng.Fori(2 - half, NI) as i:
                step(eng, layer, half, i, True, True)
            step(eng, layer, half, NI, False, True)

        CQ_HI = h_hi[:, 0:LATENT * T].rearrange("p (k t) -> p k t", t=T)
        CQ_LO = h_lo[:, 0:LATENT * T].rearrange("p (k t) -> p k t", t=T)
        CK_HI = h_hi[:, LATENT * T:LATENT * (T + TK)].rearrange("p (k t) -> p k t", t=TK)
        CK_LO = h_lo[:, LATENT * T:LATENT * (T + TK)].rearrange("p (k t) -> p k t", t=TK)
        cache = Y[:, 9:12, :].rearrange("p k t -> p (k t)")[:, 0:LATENT * PAST].rearrange("p (k t) -> p k t", t=PAST)
        kpe = Y[:, 12:14, :].rearrange("p k t -> p (k t)")[:, 0:TK]
        m = {n: sem("m_" + n) for n in [
            "cache_in", "squared", "summed", "scaled", "hi", "latents", "swapped_k", "kpe_parts", "kpe_ready", "out_dma",
            "swapped", "rope_parts", "q_ready", "scores", "masked", "maxes", "bounds", "probs", "recips", "normed",
            "v_turned", "v_tok", "p_turned", "p_tok", "o_raw", "o_hi", "o_done"]}
        qn = [qraw[:], graw[:]]
        qp = vfm[:]
        kn = [lev[:, n, 0:TK] for n in range(2)]
        values = row_tiles[:, 7:10, :].rearrange("p k t -> p (k t)")
        vf = [values[:, n * TK:(n + 1) * TK] for n in range(2)]
        qr = [key[:], query[:]]
        r1, r2 = gate[:], fgate[:]
        vt = [g_f32 for g_f32 in (Y[:, 0:2, :].rearrange("p k t -> p (k t)")[:, 0:4 * P],
                                  Y[:, 2:4, :].rearrange("p k t -> p (k t)")[:, 0:4 * P])]
        PR = TP + P + PAST + TS
        pr = [Y[:, 4:6, :].rearrange("p k t -> p (k t)")[:, 0:PR], Y[:, 6:8, :].rearrange("p k t -> p (k t)")[:, 0:PR]]
        pt = [ktok[:].rearrange("p a b -> p (a b)"), vtok[:].rearrange("p a b -> p (a b)")]
        pt_s = [s_new[:, 0, 0:2 * TS], s_new[:, 1, 0:2 * TS]]
        mx = sb("mx", [P, 2, 3])
        nb = sb("nb", [P, 2, 3])
        sums = sb("sums", [P, 2, 3])
        rc = sb("rc", [P, 2, 3])
        SC = [psum[5], psum[7]]
        SS = psum[6]
        SPANS = [(0, P), (P, TP)]
        PAIR = "pairs"

        def latent_act(act):
            act.add_instruction(mybir.InstLoadActFuncSet(act_func_set_id=EXP_LN_SET, name=nc.get_next_instruction_name(),
                                                         engine=mybir.EngineType.Activation))
            done = y_count["down"][0] + 9
            act.wait_ge(y_done, done)
            for k in range(2 * LATENT):
                if k >= 2:
                    act.wait_ge(m["summed"], k - 1)
                act.activation(SQ[k % 2], Y[:, k, :], ACT.Square).then_inc(m["squared"], 1)
            for n, out in ((0, RSA), (1, RSB)):
                act.wait_ge(m["summed"], 2 * LATENT)
                act.activation(out, psum[4 + n][:, 0:T], ACT.Ln, scale=1.0 / (LATENT * P),
                               bias=eps[:, 0:1]).then_inc(m["scaled"], 1)
                act.wait_ge(m["scaled"], 2 * n + 1)
                act.activation(out, out, ACT.Exp, scale=-0.5).then_inc(m["scaled"], 1)
            act.wait_ge(m["cache_in"], 16 * (LATENT + 2))
            act.activation(CK_HI[:, :, TP:TP + PAST], cache, ACT.Copy).then_inc(m["hi"], 1)
            for k in range(2 * LATENT):
                act.wait_ge(m["scaled"], 4 + k + 1)
                if k < LATENT:
                    act.activation(CQ_HI[:, k, :], Y[:, k, :], ACT.Copy).then_inc(m["hi"], 1)
                else:
                    act.activation(CK_HI[:, k - LATENT, 0:TP], Y[:, k, 0:TP], ACT.Copy)
                    act.activation(CK_HI[:, k - LATENT, TP + PAST:TK], Y[:, k, TP:T], ACT.Copy).then_inc(m["hi"], 1)

        def latent_pe(pe):
            for k in range(2 * LATENT):
                n = k // LATENT
                pe.wait_ge(m["squared"], k + 1)
                pe.matmul(psum[4 + n][:, 0:T], ones[:], SQ[k % 2], start=(k % LATENT == 0),
                          stop=(k % LATENT == LATENT - 1)).then_inc(m["summed"], 1)
            pe.wait_ge(y_done, y_count["down"][0] + 9)
            pe.matmul(psum[6][:, 0:T], swap[:], Y[:, 2 * LATENT, :], start=True, stop=True).then_inc(m["swapped_k"], 1)

        def latent_dve(dve):
            for n in range(2):
                dve.memset(qr[n], 0.0)
            dve.memset(mx[:], 0.0)
            dve.memset(sums[:], 1.0).then_inc(filled, 1)
            dve.wait_ge(m["scaled"], 4)
            for k in range(2 * LATENT):
                dve.scalar_tensor_tensor(out=Y[:, k, :], in0=Y[:, k, :], scalar=lat_w[:, k // LATENT, k % LATENT:k % LATENT + 1],
                                         in1=RSA if k < LATENT else RSB, op0=ALU.mult, op1=ALU.mult).then_inc(m["scaled"], 1)
            dve.wait_ge(m["hi"], 1)
            dve.tensor_tensor(CK_LO[:, :, TP:TP + PAST], cache, CK_HI[:, :, TP:TP + PAST].bitcast(F32), ALU.subtract)
            for k in range(2 * LATENT):
                dve.wait_ge(m["hi"], k + 2)
                if k < LATENT:
                    dve.tensor_tensor(CQ_LO[:, k, :], Y[:, k, :], CQ_HI[:, k, :].bitcast(F32), ALU.subtract)
                else:
                    kk = k - LATENT
                    dve.tensor_tensor(CK_LO[:, kk, 0:TP], Y[:, k, 0:TP], CK_HI[:, kk, 0:TP].bitcast(F32), ALU.subtract)
                    z = dve.tensor_tensor(CK_LO[:, kk, TP + PAST:TK], Y[:, k, TP:T], CK_HI[:, kk, TP + PAST:TK].bitcast(F32),
                                          ALU.subtract)
            z.then_inc(m["latents"], 1)
            dve.wait_ge(m["swapped_k"], 1)
            dve.tensor_tensor(r1, Y[:, 2 * LATENT, :], cos[:], ALU.mult)
            dve.tensor_tensor(r2, psum[6][:, 0:T], sin[:], ALU.mult).then_inc(m["kpe_parts"], 1)
            dve.wait_ge(m["kpe_parts"], 1)
            dve.tensor_tensor(kpe[:, 0:TP], r1[:, 0:TP], r2[:, 0:TP], ALU.add)
            dve.tensor_tensor(kpe[:, TP + PAST:TK], r1[:, TP:T], r2[:, TP:T], ALU.add).then_inc(m["kpe_ready"], 1)

        def pair_gemm(pe, j, k):
            ch = Chunk(PAIR, j, k)
            pe.wait_ge(lo_done, ch.number + 1)
            tiles = {0: [0, 1], 1: [2], 2: [3, 4], 3: [5, 6]}[k]
            for n, t in enumerate(tiles):
                if not (isinstance(j, int) and j == 0 and t < 4):
                    pe.wait_ge(evacuated, tile_number(PAIR, j, t) - 2)
                if t in (2, 3) and not (isinstance(j, int) and j == 0):
                    pe.wait_ge(m["v_tok"], 2 * j)
                width, hi, lo = (T, CQ_HI, CQ_LO) if t < 3 else (TK, CK_HI, CK_LO)
                for u in range(LATENT):
                    mm = product(pe, psum[t % 4][:, 0:width], ch, n * LATENT + u, hi[:, u, :], lo[:, u, :],
                                 u == 0, u == LATENT - 1)
            mm.then_inc(chunk_done, 1)

        def pair_evac(act, j, ts):
            dst = {0: qn[0], 1: qn[1], 2: qp, 3: kn[0], 4: kn[1], 5: vf[0], 6: vf[1]}
            for t in ts:
                act.wait_ge(chunk_done, Chunk(PAIR, j, {0: 0, 1: 0, 2: 1, 3: 2, 4: 2, 5: 3, 6: 3}[t]).number + 1)
                act.activation(dst[t], psum[t % 4][:, 0:T if t < 3 else TK], ACT.Copy).then_inc(evacuated, 1)

        def pair_act(act, j, gemm, attn, ahead):
            r = j - 1

            def turned_probs(n):
                if attn:
                    act.wait_ge(m["p_turned"], 2 * r + n + 1)
                    act.activation(pt[n], SC[n][:, 0:3 * P], ACT.Copy)
                    act.activation(pt_s[n][:, 0:TS], SC[n][:, 3 * P:3 * P + TS], ACT.Copy)
                    act.activation(pt_s[n][0:TS, TS:2 * TS], SC[n][0:TS, 3 * P + TS:3 * P + 2 * TS], ACT.Copy)\
                        .then_inc(m["p_tok"], 1)

            def out_hi(n):
                if attn:
                    act.wait_ge(m["o_raw"], 2 * r + n + 1)
                    act.activation(o_hi[:, bass.ds(2 * r + n, 1), :], (psum[6], psum[4])[n][:, 0:T].unsqueeze(1), ACT.Copy)\
                        .then_inc(m["o_hi"], 1)

            if attn:
                for n in range(2):
                    act.wait_ge(m["v_turned"], 2 * r + n + 1)
                    bank = psum[3 - n]
                    act.activation(vt[n][:, 0:3 * P], bank[:, 0:3 * P], ACT.Copy)
                    act.activation(vt[n][0:TS, 3 * P:4 * P], bank[0:TS, 3 * P:4 * P], ACT.Copy).then_inc(m["v_tok"], 1)
                for n in range(2):
                    act.wait_ge(m["bounds"], 2 * r + n + 1)
                    for tile, (c0, cn) in enumerate(SPANS):
                        act.activation(pr[n][:, c0:c0 + cn], pr[n][:, c0:c0 + cn], ACT.Exp, bias=nb[:, n, tile:tile + 1],
                                       scale=SCALE, accum_out=sums[:, n, tile:tile + 1])
                for n in range(2):
                    act.activation(pr[n][0:TS, 3 * P:PR], SS[0:TS, n * 160:n * 160 + 160], ACT.Exp, bias=nb[0:TS, n, 2:3],
                                   scale=SCALE, accum_out=sums[0:TS, n, 2:3]).then_inc(m["probs"], 1)
            for k, tiles in enumerate(([0, 1], [2], [3, 4], [5, 6])):
                if k == 1:
                    turned_probs(0)
                if k == 2:
                    turned_probs(1)
                    out_hi(0)
                if k == 3:
                    out_hi(1)
                if gemm:
                    pair_evac(act, j, tiles)
                if ahead:
                    split_hi(act, PAIR, j + 1, k)
                else:
                    split_hi(act, "mla_out", 0, k + (0 if gemm else 4))

        def pair_dve(dve, j, gemm, attn, ahead):
            r = j - 1
            if attn:
                dve.wait_ge(m["scores"], 2 * r + 2)
                for n in range(2):
                    dve.tensor_tensor(pr[n][:, 0:3 * P], SC[n][:, 0:3 * P], chunk_mask[:], ALU.add).then_inc(m["masked"], 1)
                    dve.tensor_reduce(mx[0:TS, n, 2:3], SS[0:TS, n * 160:n * 160 + 160], AX_X, ALU.max)
                    dve.wait_ge(m["masked"], 2 * r + n + 1)
                    for tile, (c0, cn) in enumerate(SPANS):
                        z = dve.tensor_reduce(mx[:, n, tile:tile + 1], pr[n][:, c0:c0 + cn], AX_X, ALU.max)
                    z.then_inc(m["maxes"], 1)
                    dve.wait_ge(m["maxes"], 2 * r + n + 1)
                    dve.tensor_scalar(nb[:, n, :], mx[:, n, :], -SCALE, None, ALU.mult).then_inc(m["bounds"], 1)
                for n in range(2):
                    dve.wait_ge(m["probs"], 2 * r + n + 1)
                    dve.reciprocal(rc[:, n, :], sums[:, n, :]).then_inc(m["recips"], 1)
                    dve.wait_ge(m["recips"], 2 * r + n + 1)
                    for tile, (c0, cn) in enumerate(SPANS):
                        dve.tensor_scalar(pr[n][:, c0:c0 + cn], pr[n][:, c0:c0 + cn], rc[:, n, tile:tile + 1], None, ALU.mult)
                    dve.tensor_scalar(pr[n][0:TS, 3 * P:PR], pr[n][0:TS, 3 * P:PR], rc[0:TS, n, 2:3], None, ALU.mult)\
                        .then_inc(m["normed"], 1)
            for k in range(4):
                if k == 2 and attn:
                    for n, bank in enumerate((psum[6], psum[4])):
                        dve.wait_ge(m["o_hi"], 2 * r + n + 1)
                        at = bass.ds(2 * r + n, 1)
                        dve.tensor_tensor(o_lo[:, at, :], bank[:, 0:T].unsqueeze(1), o_hi[:, at, :].bitcast(F32),
                                          ALU.subtract).then_inc(m["o_done"], 1)
                if k == 2 and gemm:
                    dve.wait_ge(m["swapped"], j + 1)
                    dve.tensor_tensor(r1, qp, cos[:], ALU.mult)
                    dve.tensor_tensor(r2, psum[4][:, 0:T], sin[:], ALU.mult).then_inc(m["rope_parts"], 1)
                    dve.wait_ge(m["rope_parts"], j + 1)
                    for n in range(2):
                        h = slice(64 * n, 64 * n + 64)
                        z = dve.tensor_tensor(qr[n][h, :], r1[h, :], r2[h, :], ALU.add)
                    z.then_inc(m["q_ready"], 1)
                if ahead:
                    split_lo(dve, PAIR, j + 1, k)
                else:
                    split_lo(dve, "mla_out", 0, k + (0 if gemm else 4))

        def pair_pe(pe, j, gemm, attn, ahead):
            r = j - 1

            def turn(n):
                if attn:
                    pe.wait_ge(m["normed"], 2 * r + n + 1)
                    bank = SC[n]
                    for c in range(3):
                        pe.transpose(bank[:, c * P:(c + 1) * P], pr[n][:, c * P:(c + 1) * P], ident[:])
                    pe.transpose(bank[:, 3 * P:3 * P + TS], pr[n][0:TS, 3 * P:4 * P], ident[0:TS, 0:TS])
                    pe.transpose(bank[0:TS, 3 * P + TS:3 * P + 2 * TS], pr[n][0:TS, 4 * P:PR], ident[0:TS, 0:TS])\
                        .then_inc(m["p_turned"], 1)

            def outputs(n):
                if attn:
                    pe.wait_ge(m["p_tok"], 2 * r + n + 1)
                    pe.wait_ge(m["v_tok"], 2 * r + 2)
                    bank = (psum[6], psum[4])[n]
                    v = [vt[n][:, c * P:(c + 1) * P] for c in range(3)]
                    pe.matmul(bank[:, 0:P], v[0], pt[n][:, 0:P], start=True, stop=True)
                    pe.matmul(bank[:, P:TP], v[0], pt[n][:, P:2 * P], start=True, stop=False)
                    pe.matmul(bank[:, P:TP], v[1], pt[n][:, 2 * P:3 * P], start=False, stop=True)
                    pe.matmul(bank[:, TP:T], v[2], pt_s[n][:, 0:TS], start=True, stop=False)
                    pe.matmul(bank[:, TP:T], vt[n][0:TS, 3 * P:4 * P], pt_s[n][0:TS, TS:2 * TS], start=False,
                              stop=True).then_inc(m["o_raw"], 1)

            def late(part):
                gemm_late(pe, "mla_out", part, o_hi, o_lo, m["o_done"], (HEADS - 2, HEADS - 1, HEADS))

            if not gemm:
                late(0)
                turn(0)
                late(1)
                turn(1)
                outputs(0)
                pe.wait_ge(m["v_tok"], HEADS)
                late(2)
                outputs(1)
                for part in range(3, 10):
                    late(part)
                return
            pair_gemm(pe, j, 0)
            turn(0)
            pair_gemm(pe, j, 1)
            turn(1)
            outputs(0)
            pair_gemm(pe, j, 2)
            outputs(1)
            if gemm:
                if attn:
                    pe.wait_ge(m["o_done"], 2 * r + 2)
                pe.wait_ge(evacuated, tile_number(PAIR, j, 2) + 1)
                pe.matmul(psum[4][:, 0:T], swap[:], qp, start=True, stop=True).then_inc(m["swapped"], 1)
                pair_gemm(pe, j, 3)
                pe.wait_ge(m["q_ready"], j + 1)
                pe.wait_ge(evacuated, tile_number(PAIR, j, 4) + 1)
                for n in range(2):
                    for c0, q0, k0, kn_ in ((0, 0, 0, P), (P, P, 0, TP)):
                        out = SC[n][:, c0:c0 + kn_]
                        pe.matmul(out, qn[n][:, q0:q0 + P], kn[n][:, k0:k0 + kn_], start=True, stop=False)
                        pe.matmul(out, qr[n][:, q0:q0 + P], kpe[:, k0:k0 + kn_], start=False, stop=True)
                    out = SS[0:TS, n * 160:n * 160 + 160]
                    pe.matmul(out, qn[n][:, TP:T], kn[n][:, TP:TK], start=True, stop=False)
                    pe.matmul(out, qr[n][:, TP:T], kpe[:, TP:TK], start=False, stop=True).then_inc(m["scores"], 1)
                for n in range(2):
                    pe.wait_ge(evacuated, tile_number(PAIR, j, 5 + n) + 1)
                    bank = psum[3 - n]
                    for c in range(4):
                        w = P if c < 3 else TS
                        tr = pe.transpose(bank[0:w, c * P:(c + 1) * P], vf[n][:, c * P:c * P + w], ident[:])
                    tr.then_inc(m["v_turned"], 1)

        def run_pairs(eng, step):
            step(eng, 0, True, False, True)
            with eng.Fori(1, PAIRS - 1) as j:
                step(eng, j, True, True, True)
            step(eng, PAIRS - 1, True, True, False)
            step(eng, PAIRS, False, True, False)

        y_out = sem("y_out")
        block = ctx.enter_context(nc.Block())

        @block.sync
        def _(sp):
            for k in range(len(CHUNKS[IN])):
                if k < 4:
                    n = KT // 4
                    sp.dma_start(X[:, k * n:(k + 1) * n, :], a["x"][:, k * n:(k + 1) * n, :]).then_inc(x_in[k], 16)
                ring_load(sp, a["w_hi_in"], IN, 0, k, chunks_of(IN, 0)[k][0])
            with sp.Fori(1, HEADS) as i:
                for k in range(len(CHUNKS[IN])):
                    ring_load(sp, a["w_hi_in"], IN, i, k, i * 4 + CHUNKS[IN][k][0])

            def load(w, phase, first):
                for k in range(len(CHUNKS[phase])):
                    ring_load(sp, w, phase, 0, k, first + chunks_of(phase, 0)[k][0])
                if TRIPS[phase] == 1:
                    return
                with sp.Fori(1, TRIPS[phase]) as i:
                    for k in range(len(CHUNKS[phase])):
                        ring_load(sp, w, phase, i, k, i * TILES[phase] + (first + CHUNKS[phase][k][0]))
            load(a["w_ho"], "hgrn_out", 0)
            for layer in range(2):
                if layer == 1:
                    load(a["w_down"], "down", 0)
                    with sp.Fori(0, PAIRS) as i:
                        for k in range(4):
                            ring_load(sp, a["w_uq"] if k < 2 else a["w_ukv"], PAIR, i, k, i)
                    load(a["w_mo"], "mla_out", 0)
                for half in range(2):
                    load(a["w_fi"], f"ffn_in{layer}{half}", (2 * layer + half) * 2 * HF)
                    load(a["w_fo"], f"ffn_out{layer}{half}", (2 * layer + half) * KT)
            sp.wait_ge(S["s_stored"], 32 * HEADS)
            for k in range(KT):
                sp.wait_ge(x_ready, KT * 3 + k + 1)
                sp.dma_start(a["o_y"][:, k, :], X[:, k, :]).then_inc(y_out, 16)
            sp.wait_ge(y_out, 16 * KT)

        @block.gpsimd
        def _(pool):
            loads = [(lbl[:], a["lbl"]), (gnorm_w[:], a["gnorm_w"]), (ident[:], a["ident"]),
                     (carry[:], a["carry"]), (level_mask_f[:], a["level_mask"]),
                     (conv_w[:], a["conv_w"]), (conv_old[:], a["conv_old"]), (lat_w[:], a["lat_w"]), (swap[:], a["swap"]),
                     (cos[:], a["cos"]), (sin[:], a["sin"]), (chunk_mask[:], a["chunk_mask"])]
            for dst, src in loads:
                pool.dma_start(dst, src).then_inc(consts_in, 16)
            pool.sem_inc(f_scaled, 4)
            norm_pool(pool, 0)
            pool.wait_ge(n_rstd, stat[0, "pre"] + 1)
            hgrn_pool(pool, 0)
            with pool.Fori(1, HEADS) as j:
                hgrn_pool(pool, j)
            norm_pool(pool, 1)
            pool.wait_ge(consts_in, 16 * len(loads))
            for layer in range(2):
                if layer == 1:
                    pool.wait_ge(h_ready, 3 * KT)
                    pool.dma_start(cache, a["cache"]).then_inc(m["cache_in"], 16 * LATENT)
                    for n in range(2):
                        pool.dma_start(kpe[64 * n:64 * n + 64, TP:TP + PAST], a["cache_kpe"]).then_inc(m["cache_in"], 16)
                    pool.wait_ge(m["scaled"], 4 + 2 * LATENT)
                    pool.dma_start(a["o_ckv"], Y[:, LATENT:2 * LATENT, :]).then_inc(m["out_dma"], 16)
                    pool.wait_ge(m["kpe_ready"], 1)
                    pool.dma_start(a["o_kpe"][:, 0:TP], kpe[0:64, 0:TP]).then_inc(m["out_dma"], 16)
                    pool.dma_start(a["o_kpe"][:, TP:T], kpe[0:64, TP + PAST:TK]).then_inc(m["out_dma"], 16)
                    pool.wait_ge(m["out_dma"], 48)
                    pool.wait_ge(conv_stored, 16)
                    norm_pool(pool, 3)
                for half in range(2):
                    if half == 0:
                        pool.wait_ge(n_rstd, stat[2 * layer + 1, "pre"] + 1)
                    ffn_pool(pool, layer, half, 0)
                    with pool.Fori(1, NI) as i:
                        ffn_pool(pool, layer, half, i)
                if layer == 0:
                    norm_pool(pool, 2)
                pool.wait_ge(rows_done, (layer + 1) * NI * 8)
                pool.dma_start(a["o_conv"][layer], conv_new[:]).then_inc(conv_stored, 16)
            pool.wait_ge(conv_stored, 32)

        @block.scalar
        def _(act):
            act.dma_start(norm_w[:], a["norm_w"]).then_inc(norm_w_in, 16)
            state_load(act, 0)
            for k in range(4):
                split_hi(act, IN, 0, k)
            act.wait_ge(filled, 1)
            act.wait_ge(norm_w_in, 16)
            norm_act(act, 0)

            def first(act):
                for k in range(4, 8):
                    split_hi(act, IN, 0, k)
                act.wait_ge(S["lb_ready"], 1)
                act.activation(lbt[:, 0:3, :], lbt[:, 0:3, :], ACT.Exp).then_inc(S["lb_ready"], 1)
                pre_stat_act(act, 0)
                act.wait_ge(chunk_done, last_chunk(IN, 0, 0))
                act.activation(HG.EX[:, 0:T], psum[0][:, 0:T], ACT.Copy).then_inc(evacuated, 1)
                act.wait_ge(chunk_done, last_chunk(IN, 0, 1))
                act.activation(qraw[:], psum[1][:, 0:T], ACT.Copy).then_inc(evacuated, 1)
            run_hgrn(act, hgrn_act, first)
            run_out_act(act, "hgrn_out")
            norm_act(act, 1)
            for layer in range(2):
                if layer == 1:
                    run_out_act(act, "down", lambda e: pre_stat_act(e, 2))
                    latent_act(act)
                    act.wait_ge(m["latents"], 1)
                    run_pairs(act, pair_act)
                    run_out_act(act, "mla_out")
                    norm_act(act, 3)
                for half in range(2):
                    run_ffn_in(act, ffn_act, layer, half)
                    run_out_act(act, f"ffn_out{layer}{half}")
                norm_act(act, 2 if layer == 0 else 4)

        @block.vector
        def _(dve):
            dve.memset(ones[:], 1.0).then_inc(y_done, 4)
            dve.memset(eps[:], EPS).then_inc(filled, 1)
            for k in range(4):
                split_lo(dve, IN, 0, k)
            dve.wait_ge(norm_w_in, 16)
            norm_dve(dve, 0)
            steps = sem("lb_steps")

            def first(dve):
                for k in range(4, 8):
                    split_lo(dve, IN, 0, k)
                dve.wait_ge(consts_in, 16 * 12)
                dve.tensor_tensor(lbt[:, 3, :], lbl[:, 0, :], lbl[:, 1, :], ALU.max).then_inc(steps, 1)
                dve.wait_ge(steps, 1)
                dve.tensor_tensor(lbt[:, 3, :], lbt[:, 3, :], lbl[:, 2, :], ALU.max).then_inc(steps, 1)
                dve.wait_ge(steps, 2)
                for n in range(3):
                    z = dve.tensor_tensor(lbt[:, n, :], lbl[:, n, :], lbt[:, 3, :], ALU.subtract)
                z.then_inc(S["lb_ready"], 1)
                dve.wait_ge(S["lb_ready"], 2)
                dve.tensor_tensor(lbt[:, 1, :], lbt[:, 1, :], lbt[:, 2, :], ALU.add).then_inc(steps, 1)
                dve.wait_ge(steps, 3)
                dve.tensor_tensor(lbt[:, 3, :], lbt[:, 0, :], lbt[:, 1, :], ALU.add).then_inc(steps, 1)
                dve.wait_ge(steps, 4)
                dve.reciprocal(lbt[:, 3, :], lbt[:, 3, :]).then_inc(steps, 1)
                dve.wait_ge(steps, 5)
                dve.tensor_tensor(lb[:], lbt[:, 0, :], lbt[:, 3, :], ALU.mult)
                dve.tensor_tensor(oml[:], lbt[:, 1, :], lbt[:, 3, :], ALU.mult).then_inc(steps, 1)
                dve.wait_ge(steps, 6)
            run_hgrn(dve, hgrn_dve, first)
            run_out_dve(dve, "hgrn_out")
            dve.wait_ge(S["s_stored"], 32 * HEADS)
            dve.memset(ext[:, :, 0:2], 0.0).then_inc(conv_done, 4)
            norm_dve(dve, 1)
            for layer in range(2):
                if layer == 1:
                    run_out_dve(dve, "down")
                    latent_dve(dve)
                    dve.wait_ge(m["out_dma"], 48)
                    run_pairs(dve, pair_dve)
                    run_out_dve(dve, "mla_out")
                    norm_dve(dve, 3)
                    dve.memset(ext[:, :, 0:2], 0.0)
                for half in range(2):
                    run_ffn_in(dve, ffn_dve, layer, half)
                    run_out_dve(dve, f"ffn_out{layer}{half}")
                norm_dve(dve, 2 if layer == 0 else 4)

        @block.tensor
        def _(pe):
            pe.wait_ge(filled, 1)
            run_hgrn(pe, hgrn_pe, lambda e: (gemm_first(e, IN, 0), e.wait_ge(consts_in, 16 * 12)))
            run_out_pe(pe, "hgrn_out", o_hi, o_lo, KT, 8)
            norm_pe(pe, 1)
            for layer in range(2):
                if layer == 1:
                    gemm_first(pe, "down", 2)
                    run_out_pe(pe, "down", H_HI, H_LO, KT, 8)
                    latent_pe(pe)
                    pe.wait_ge(m["latents"], 1)
                    pe.wait_ge(m["kpe_ready"], 1)
                    pe.wait_ge(m["cache_in"], 16 * (LATENT + 2))
                    run_pairs(pe, pair_pe)
                    run_out_pe(pe, "mla_out", o_hi, o_lo, KT, 8)
                    norm_pe(pe, 3)
                for half in range(2):
                    if half == 0:
                        gemm_first(pe, f"ffn_in{layer}0", 2 * layer + 1)
                    run_out_pe(pe, f"ffn_in{layer}{half}", H_HI, H_LO, KT, 8 if half == 0 else 0)
                    run_out_pe(pe, f"ffn_out{layer}{half}", g_hi, g_lo, HF, 0, (g_done, ffn_base(layer, half) * HF))
                norm_pe(pe, 2 if layer == 0 else 4)


def kernel(x_prompt, x_sample, state_hgrn, cache_ckv, cache_kpe, state_conv, norm_w, lb_logits, hgrn_w_in, hgrn_gnorm_w,
           hgrn_w_out, mla_w_down, mla_q_norm_w, mla_kv_norm_w, mla_w_uq, mla_w_ukv, mla_w_out, ffn_w_in, ffn_conv_w,
           ffn_conv_b, ffn_w_out):
    import numpy as np
    import concourse.bacc as _bacc
    from concourse.bass_utils import run_bass_kernel_spmd as _run

    f = lambda v: np.asarray(v)
    D = x_prompt.shape[-1]
    KT = D // P
    H = D // P
    FF = ffn_w_out.shape[1]
    FT = FF // P
    HF = FT // 2
    lora = LATENT * P

    def rows(w):
        return w.reshape(-1, P, w.shape[-1]).transpose(1, 0, 2)

    def tiles(w, kt=None):
        k, n = w.shape
        return w.reshape(k // P, P, n // P, P).transpose(2, 1, 0, 3).reshape(n // P, P, k)

    A = {}
    A["x"] = rows(np.concatenate([f(x_prompt)[0], f(x_sample)[0]], 0).T)
    A["s_in"] = f(state_hgrn)[0, 0]
    A["norm_w"] = f(norm_w).reshape(2, 4, KT, P).transpose(3, 0, 1, 2)
    A["lbl"] = f(lb_logits).reshape(3, KT, P).transpose(2, 0, 1)
    A["gnorm_w"] = f(hgrn_gnorm_w)[0][:, None]
    w = tiles(f(hgrn_w_in)[0]).reshape(4, H, P, D)
    A["w_hi_in"] = w[[1, 0, 2, 3]].transpose(1, 0, 2, 3).reshape(4 * H, P, D)
    A["w_ho"] = tiles(f(hgrn_w_out)[0])
    w = f(mla_w_down)[0]
    A["w_down"] = tiles(np.concatenate([w, w[:, 2 * lora:]], 1))
    uq = f(mla_w_uq)[0].reshape(lora, H, 192)
    nope = tiles(uq[:, :, :128].reshape(lora, H * P)).reshape(H // 2, 2, P, lora)
    pe_ = tiles(uq[:, :, 128:].reshape(lora, H * 64)).reshape(H // 2, 1, P, lora)
    A["w_uq"] = np.concatenate([nope, pe_], 1).transpose(0, 2, 1, 3).reshape(H // 2, P, 3 * lora)
    ukv = f(mla_w_ukv)[0].reshape(lora, H, 2, P)
    kv = [tiles(ukv[:, :, n].reshape(lora, H * P)).reshape(H // 2, 2, P, lora) for n in range(2)]
    A["w_ukv"] = np.concatenate(kv, 1).transpose(0, 2, 1, 3).reshape(H // 2, P, 4 * lora)
    A["w_mo"] = tiles(f(mla_w_out)[0])
    fi = f(ffn_w_in)
    A["w_fi"] = np.concatenate([tiles(fi[l]).reshape(2, FT, P, D).transpose(1, 0, 2, 3).reshape(2 * FT, P, D)
                                for l in range(2)], 0)
    fo = f(ffn_w_out)
    A["w_fo"] = np.concatenate([tiles(fo[l, h * HF * P:(h + 1) * HF * P]) for l in range(2) for h in range(2)], 0)
    A["w_fo"] = A["w_fo"].reshape(4 * KT, P, HF * P)
    taps = np.concatenate([f(ffn_conv_w), f(ffn_conv_b)[:, None]], 1)
    A["conv_w"] = taps.reshape(2, 4, 2, FT, P).transpose(4, 0, 3, 2, 1).reshape(P, 2, 2 * FT, 4)
    A["conv_old"] = f(state_conv)[:, 0].reshape(2, 2, 2, FT, P).transpose(4, 0, 3, 2, 1).reshape(P, 2, 2 * FT, 2)
    A["lat_w"] = np.stack([f(mla_q_norm_w)[0], f(mla_kv_norm_w)[0]]).reshape(2, LATENT, P).transpose(2, 0, 1)
    A["cache"] = rows(f(cache_ckv)[0, 0].T)
    A["cache_kpe"] = f(cache_kpe)[0, 0].T
    A["ident"] = np.eye(P, dtype=np.float32)
    p = np.arange(P)
    A["swap"] = (p[:, None] == (p ^ 32)[None]).astype(np.float32)
    pos = np.concatenate([np.arange(TP), PAST + np.arange(TS)]).astype(np.float32)
    inv = (np.float32(10000.0) ** (-np.arange(32, dtype=np.float32) / np.float32(32))).astype(np.float32)
    ang = (pos[None] * inv[p % 32][:, None]).astype(np.float32)
    A["cos"] = np.cos(ang).astype(np.float32)
    A["sin"] = (np.sin(ang) * np.where(p % 64 < 32, -1, 1)[:, None]).astype(np.float32)
    q = np.arange(P)[:, None]
    A["chunk_mask"] = np.concatenate([np.where(np.arange(P)[None] // 64 > q // 64, NEGATIVE, 0),
                                      np.where(np.arange(TP)[None] // 64 > (q + P) // 64, NEGATIVE, 0)], 1).astype(np.float32)
    lm = np.zeros((P, LEVELS, 64), np.float32)
    for l in range(LEVELS):
        half = 2 ** l
        b = np.arange(64) // half
        lm[:, l] = (p[:, None] // half == 2 * b[None])
    A["level_mask"] = lm
    carry = np.ones((P, T), np.float32)
    carry[:, [0, P, TP]] = 0
    A["carry"] = carry

    outs = {"o_y": (P, KT, T), "o_hp": (H, P, P), "o_hs": (H, P, P), "o_ckv": (P, LATENT, T), "o_kpe": (64, T),
            "o_conv": (2, P, 2 * FT, 4)}
    nc = _bacc.Bacc("TRN2", target_bir_lowering=False, num_devices=1)
    arrays, args = {}, {}
    for name, v in A.items():
        v = np.ascontiguousarray(v)
        arrays["in_" + name] = v
        args[name] = nc.dram_tensor("in_" + name, v.shape, mybir.dt.from_np(v.dtype), kind="ExternalInput").ap()
    for name, shape in outs.items():
        args[name] = nc.dram_tensor(name, shape, F32, kind="ExternalOutput").ap()
    trunk_program(nc, args)
    got = _run(nc, [arrays], core_ids=[0]).results[0]

    y = got["o_y"].transpose(2, 1, 0).reshape(T, D)
    ckv = got["o_ckv"].transpose(2, 1, 0).reshape(T, lora)
    kpe = got["o_kpe"].T
    conv = got["o_conv"].reshape(2, P, FT, 2, 2, 2).transpose(0, 4, 5, 3, 2, 1).reshape(2, 2, 2, 2 * FF)
    return (y[None, :TP], y[None, TP:], got["o_hp"][None, None], got["o_hs"][None, None],
            ckv[None, None, :TP], ckv[None, None, TP:], kpe[None, None, :TP], kpe[None, None, TP:],
            conv[:, 0][:, None], conv[:, 1][:, None])
```
